# Optimizing a Trainium2 kernel written in Bass

```python
import math
import jax, jax.numpy as jnp
from jax import lax
import numpy as np

D_MODEL = 1024
BATCH = 1
SEQ = 512
DEPTH = 2

N_A_LAYERS = DEPTH // 2
N_B_LAYERS = DEPTH - N_A_LAYERS
HEAD_DIM = 128
GDN_HEADS = 6
GDN_WIDTH = GDN_HEADS * HEAD_DIM
CONV_WIDTH = 4
CHUNK = 64
FOX_HEADS = 6
FOX_WIDTH = FOX_HEADS * HEAD_DIM
Q_BLOCK = 128
MEM_LEN = 256
MEM_HEADS = 4
MEM_HEAD_DIM = 64
MEM_WIDTH = MEM_HEADS * MEM_HEAD_DIM
MIX_WIDTH = GDN_WIDTH + MEM_WIDTH
A_IN_WIDTH = 4 * GDN_WIDTH + 2 * GDN_HEADS + MEM_WIDTH
B_IN_WIDTH = FOX_WIDTH + MEM_WIDTH
KV_WIDTH = 2 * FOX_WIDTH + FOX_HEADS
FFN_HIDDEN = 2816
EPS = 1e-6
NEG_INF = -1e30

kernel_name = "yoco_gdn_fox_macaron_memory"

def rmsnorm(x, gain):
    x32 = x.astype(jnp.float32)
    y = x32 * lax.rsqrt(jnp.mean(x32 * x32, axis=-1, keepdims=True) + EPS)
    return (y * gain.astype(jnp.float32)).astype(x.dtype)

def l2norm(x):
    x32 = x.astype(jnp.float32)
    return x32 * lax.rsqrt(jnp.sum(x32 * x32, axis=-1, keepdims=True) + EPS)

def swiglu(x, w_gate_up, w_down):
    gate, up = jnp.split(x @ w_gate_up, 2, axis=-1)
    return (jax.nn.silu(gate) * up) @ w_down

def causal_depthwise_conv(x, w):
    c = x.shape[-1]
    return lax.conv_general_dilated(
        x, w[:, None, :].astype(x.dtype), window_strides=(1,),
        padding=((CONV_WIDTH - 1, 0),), dimension_numbers=("NWC", "WIO", "NWC"),
        feature_group_count=c)

def chunk_gated_delta_rule(q, k, v, g, beta):
    bsz, s, h, dk = q.shape
    dv = v.shape[-1]
    n = s // CHUNK

    def chunks(t):
        return t.reshape(bsz, n, CHUNK, h, -1).transpose(0, 3, 1, 2, 4)

    q, k, v = chunks(q), chunks(k), chunks(v)
    g = g.reshape(bsz, n, CHUNK, h).transpose(0, 3, 1, 2)
    beta = beta.reshape(bsz, n, CHUNK, h).transpose(0, 3, 1, 2)
    g = jnp.cumsum(g, axis=-1)
    causal = jnp.tril(jnp.ones((CHUNK, CHUNK), dtype=bool))
    strict = jnp.tril(jnp.ones((CHUNK, CHUNK), dtype=bool), k=-1)
    gdiff = g[..., :, None] - g[..., None, :]
    decay = jnp.where(causal, jnp.exp(jnp.where(causal, gdiff, 0.0)), 0.0)
    k_beta = k * beta[..., None]
    lower = jnp.where(strict, jnp.einsum("bhnid,bhnjd->bhnij", k_beta, k) * decay, 0.0)
    system = lower + jnp.eye(CHUNK, dtype=jnp.float32)
    rhs = jnp.concatenate([v * beta[..., None], k_beta * jnp.exp(g)[..., None]], axis=-1)
    sol = lax.linalg.triangular_solve(system, rhs, left_side=True, lower=True,
                                      unit_diagonal=True)
    u_vals, w_keys = sol[..., :dv], sol[..., dv:]
    qk = jnp.where(causal, jnp.einsum("bhnid,bhnjd->bhnij", q, k) * decay, 0.0)
    g_last = g[..., -1]
    k_tail = k * jnp.exp(g_last[..., None] - g)[..., None]
    q_head = q * jnp.exp(g)[..., None]
    xs = tuple(jnp.moveaxis(t, 2, 0) for t in (q_head, qk, u_vals, w_keys, k_tail, g_last))

    def step(state, inp):
        q_c, qk_c, u_c, w_c, kt_c, gl_c = inp
        v_new = u_c - jnp.einsum("bhck,bhkv->bhcv", w_c, state)
        out = (jnp.einsum("bhck,bhkv->bhcv", q_c, state)
               + jnp.einsum("bhij,bhjv->bhiv", qk_c, v_new))
        state = (state * jnp.exp(gl_c)[..., None, None]
                 + jnp.einsum("bhck,bhcv->bhkv", kt_c, v_new))
        return state, out

    state0 = jnp.zeros((bsz, h, dk, dv), jnp.float32)
    _, out = lax.scan(step, state0, xs)
    return out.transpose(1, 0, 3, 2, 4).reshape(bsz, s, h, dv)

def gdn_mixer(u, w_in, conv_w, A_log, dt_bias, out_norm):
    bsz, s, _ = u.shape
    proj = u @ w_in
    o0 = 3 * GDN_WIDTH
    o1 = 4 * GDN_WIDTH
    qkv = proj[..., :o0]
    z = proj[..., o0:o1]
    a = proj[..., o1:o1 + GDN_HEADS]
    b = proj[..., o1 + GDN_HEADS:o1 + 2 * GDN_HEADS]
    q_mem = proj[..., o1 + 2 * GDN_HEADS:]
    qkv = jax.nn.silu(causal_depthwise_conv(qkv, conv_w))
    qkv = qkv.reshape(bsz, s, 3, GDN_HEADS, HEAD_DIM)
    q = l2norm(qkv[:, :, 0]) * (HEAD_DIM ** -0.5)
    k = l2norm(qkv[:, :, 1])
    v = qkv[:, :, 2].astype(jnp.float32)
    beta = jax.nn.sigmoid(b.astype(jnp.float32))
    g = -jnp.exp(A_log.astype(jnp.float32)) * jax.nn.softplus(
        a.astype(jnp.float32) + dt_bias.astype(jnp.float32))
    o = chunk_gated_delta_rule(q, k, v, g, beta)
    z = z.reshape(bsz, s, GDN_HEADS, HEAD_DIM).astype(jnp.float32)
    o = rmsnorm(o, out_norm) * jax.nn.silu(z)
    return o.reshape(bsz, s, GDN_WIDTH).astype(u.dtype), q_mem

def shared_fox_kv(h, kv_norm, kv_w, kv_b_f):
    bsz, s, _ = h.shape
    p = rmsnorm(h, kv_norm) @ kv_w
    k = p[..., :FOX_WIDTH].reshape(bsz, s, FOX_HEADS, HEAD_DIM)
    v = p[..., FOX_WIDTH:2 * FOX_WIDTH].reshape(bsz, s, FOX_HEADS, HEAD_DIM)
    log_f = jax.nn.log_sigmoid(p[..., 2 * FOX_WIDTH:].astype(jnp.float32)
                               + kv_b_f.astype(jnp.float32))
    c = jnp.cumsum(log_f, axis=1).transpose(0, 2, 1)
    return k, v, c

def forgetting_attention(q, k, v, c):
    bsz, s, h, d = q.shape
    nb = s // Q_BLOCK
    scale = d ** -0.5
    q_blocks = q.reshape(bsz, nb, Q_BLOCK, h, d).transpose(1, 0, 3, 2, 4)
    c_blocks = c.reshape(bsz, h, nb, Q_BLOCK).transpose(2, 0, 1, 3)
    key_pos = jnp.arange(s)

    def attend(args):
        q_i, c_i, i = args
        logits = jnp.einsum("bhqd,bshd->bhqs", q_i, k).astype(jnp.float32) * scale
        logits = logits + c_i[..., None] - c[:, :, None, :]
        q_pos = i * Q_BLOCK + jnp.arange(Q_BLOCK)
        causal = key_pos[None, :] <= q_pos[:, None]
        p = jax.nn.softmax(jnp.where(causal, logits, NEG_INF), axis=-1)
        return jnp.einsum("bhqs,bshd->bqhd", p.astype(v.dtype), v)

    out = lax.map(attend, (q_blocks, c_blocks, jnp.arange(nb)))
    return out.transpose(1, 0, 2, 3, 4).reshape(bsz, s, h * d).astype(q.dtype)

def memory_attention(q, mem_n, w_kv):
    bsz, s, _ = q.shape
    m = mem_n.shape[1]
    kv = mem_n @ w_kv
    k = kv[..., :MEM_WIDTH].reshape(bsz, m, MEM_HEADS, MEM_HEAD_DIM)
    v = kv[..., MEM_WIDTH:].reshape(bsz, m, MEM_HEADS, MEM_HEAD_DIM)
    q = q.reshape(bsz, s, MEM_HEADS, MEM_HEAD_DIM)
    logits = jnp.einsum("bqhd,bmhd->bhqm", q, k).astype(jnp.float32) * (MEM_HEAD_DIM ** -0.5)
    p = jax.nn.softmax(logits, axis=-1)
    out = jnp.einsum("bhqm,bmhd->bqhd", p.astype(v.dtype), v)
    return out.reshape(bsz, s, MEM_WIDTH)

def setup_inputs(seed: int = 0) -> dict:
    key = jax.random.key(seed)
    ks = iter(jax.random.split(key, 32))

    def nrm(shape, scale):
        return scale * jax.random.normal(next(ks), shape, jnp.float32)

    def gain(shape):
        return 1.0 + nrm(shape, 0.02)

    x = nrm((BATCH, SEQ, D_MODEL), 1.0)
    mem = nrm((BATCH, MEM_LEN, D_MODEL), 1.0)
    ffn1_norm = gain((DEPTH, D_MODEL))
    ffn1_w_gate_up = nrm((DEPTH, D_MODEL, 2 * FFN_HIDDEN), D_MODEL ** -0.5)
    ffn1_w_down = nrm((DEPTH, FFN_HIDDEN, D_MODEL), FFN_HIDDEN ** -0.5)
    mix_norm = gain((DEPTH, D_MODEL))
    ffn2_norm = gain((DEPTH, D_MODEL))
    ffn2_w_gate_up = nrm((DEPTH, D_MODEL, 2 * FFN_HIDDEN), D_MODEL ** -0.5)
    ffn2_w_down = nrm((DEPTH, FFN_HIDDEN, D_MODEL), FFN_HIDDEN ** -0.5)
    gdn_w_in = nrm((N_A_LAYERS, D_MODEL, A_IN_WIDTH), D_MODEL ** -0.5)
    gdn_conv = nrm((N_A_LAYERS, CONV_WIDTH, 3 * GDN_WIDTH), CONV_WIDTH ** -0.5)
    gdn_A_log = jnp.log(jax.random.uniform(next(ks), (N_A_LAYERS, GDN_HEADS),
                                           jnp.float32, 1.0, 16.0))
    dt = jnp.exp(jax.random.uniform(next(ks), (N_A_LAYERS, GDN_HEADS), jnp.float32,
                                    math.log(1e-3), math.log(1e-1)))
    gdn_dt_bias = dt + jnp.log(-jnp.expm1(-dt))
    gdn_out_norm = gain((N_A_LAYERS, HEAD_DIM))
    fox_w_in = nrm((N_B_LAYERS, D_MODEL, B_IN_WIDTH), D_MODEL ** -0.5)
    w_out = nrm((DEPTH, MIX_WIDTH, D_MODEL), MIX_WIDTH ** -0.5)
    mem_norm = gain((D_MODEL,))
    mem_w_kv = nrm((DEPTH, D_MODEL, 2 * MEM_WIDTH), D_MODEL ** -0.5)
    kv_norm = gain((D_MODEL,))
    kv_w = nrm((D_MODEL, KV_WIDTH), D_MODEL ** -0.5)
    kv_b_f = 2.0 + nrm((FOX_HEADS,), 0.1)
    final_norm = gain((D_MODEL,))
    return {"x": x, "mem": mem,
            "ffn1_norm": ffn1_norm, "ffn1_w_gate_up": ffn1_w_gate_up, "ffn1_w_down": ffn1_w_down,
            "mix_norm": mix_norm,
            "ffn2_norm": ffn2_norm, "ffn2_w_gate_up": ffn2_w_gate_up, "ffn2_w_down": ffn2_w_down,
            "gdn_w_in": gdn_w_in, "gdn_conv": gdn_conv, "gdn_A_log": gdn_A_log,
            "gdn_dt_bias": gdn_dt_bias, "gdn_out_norm": gdn_out_norm,
            "fox_w_in": fox_w_in, "w_out": w_out,
            "mem_norm": mem_norm, "mem_w_kv": mem_w_kv,
            "kv_norm": kv_norm, "kv_w": kv_w, "kv_b_f": kv_b_f,
            "final_norm": final_norm}

def reference(x, mem, ffn1_norm, ffn1_w_gate_up, ffn1_w_down, mix_norm,
              ffn2_norm, ffn2_w_gate_up, ffn2_w_down,
              gdn_w_in, gdn_conv, gdn_A_log, gdn_dt_bias, gdn_out_norm,
              fox_w_in, w_out, mem_norm, mem_w_kv, kv_norm, kv_w, kv_b_f, final_norm):
    bsz, s, _ = x.shape
    mem_n = rmsnorm(mem, mem_norm)
    h = x
    shared_k = shared_v = shared_c = None
    for l in range(DEPTH):
        h = h + 0.5 * swiglu(rmsnorm(h, ffn1_norm[l]), ffn1_w_gate_up[l], ffn1_w_down[l])
        u = rmsnorm(h, mix_norm[l])
        if l < N_A_LAYERS:
            main, q_mem = gdn_mixer(u, gdn_w_in[l], gdn_conv[l], gdn_A_log[l],
                                    gdn_dt_bias[l], gdn_out_norm[l])
        else:
            proj = u @ fox_w_in[l - N_A_LAYERS]
            q_fox = proj[..., :FOX_WIDTH].reshape(bsz, s, FOX_HEADS, HEAD_DIM)
            q_mem = proj[..., FOX_WIDTH:]
            main = forgetting_attention(q_fox, shared_k, shared_v, shared_c)
        mem_out = memory_attention(q_mem, mem_n, mem_w_kv[l])
        h = h + jnp.concatenate([main, mem_out], axis=-1) @ w_out[l]
        h = h + 0.5 * swiglu(rmsnorm(h, ffn2_norm[l]), ffn2_w_gate_up[l], ffn2_w_down[l])
        if l == N_A_LAYERS - 1:
            shared_k, shared_v, shared_c = shared_fox_kv(h, kv_norm, kv_w, kv_b_f)
    return rmsnorm(h, final_norm)


_drawn_inputs = setup_inputs


def setup_inputs(seed=0):
    import zlib

    import numpy as np

    out = dict(_drawn_inputs(seed))
    spreads = {}
    factors = {'ffn1_norm': 4.309,
     'mix_norm': 3.13,
     'ffn2_norm': 5.444,
     'gdn_out_norm': 5.521,
     'mem_norm': 8.0,
     'kv_norm': 7.985,
     'kv_b_f': 7.737,
     'final_norm': 2.75}
    for name, (base, spread) in spreads.items():
        noise = np.random.default_rng([zlib.crc32(name.encode()), seed]).standard_normal(out[name].shape)
        drawn = base * np.exp(spread * noise) if base else spread * noise
        out[name] = __import__('jax').numpy.asarray(drawn.astype(out[name].dtype))
    for name, factor in factors.items():
        out[name] = (out[name] * factor).astype(out[name].dtype)
    return out
```

```python
from contextlib import ExitStack

import concourse.bass as bass
from concourse import mybir

F32 = mybir.dt.float32
F32R = mybir.dt.float32r
ALU = mybir.AluOpType
ACT = mybir.ActivationFunctionType
AX_X = mybir.AxisListType.X

P = 128
D_MODEL = 1024
SEQ = 512
DEPTH = 2
HEAD = 128
HEADS = 6
WIDTH = HEADS * HEAD
CONV = 4
CHUNK = 64
MEM_LEN = 256
MEM_HEADS = 4
MEM_HEAD = 64
MEM_WIDTH = MEM_HEADS * MEM_HEAD
FFN = 2816
EPS = 1e-6
NEG_INF = -1e30

KT = D_MODEL // P
TT = SEQ // P
MT = MEM_LEN // P
NP = FFN // P
HALF = NP // 2
FULL_UNIT = KT * 2 * P
DOWN_UNIT = HALF * P
ROW_B = 32

G_FFN1, G_MIX, G_FFN2, G_KV, G_FINAL, G_MEM = 0, 2 * KT, 4 * KT, 6 * KT, 7 * KT, 8 * KT
G_OUT = 9 * KT
GAINS = 9 * KT + 1


def unit_plan(phases):
    first_unit, first_group, sizes = {}, {}, []
    group = 0
    for name in phases:
        kind = name.rstrip("0123456789")
        first_unit[name], first_group[name] = len(sizes), group
        if kind == "memtr":
            group += KT
        elif kind == "memkv":
            sizes += [FULL_UNIT] * 2
            group += 2
        elif kind == "memvtr":
            group += DEPTH
        elif kind == "xtr":
            group += KT
        elif kind == "up":
            sizes += [FULL_UNIT] * NP
            group += NP
        elif kind == "down":
            sizes += [DOWN_UNIT] * (2 * KT)
            group += KT
        elif kind == "gdnin":
            sizes += [KT * P] + [FULL_UNIT] * 13
            group += 14
        elif kind == "foxin":
            sizes += [FULL_UNIT] * 4
            group += 4
        elif kind == "wout":
            sizes += [FULL_UNIT] * (KT // 2)
            group += KT // 2
        elif kind == "kv":
            sizes += [KT * P] + [FULL_UNIT] * HEADS
            group += 1 + HEADS
    return first_unit, first_group, sizes


def build_trunk(nc, mem, x, ffn1_norm, ffn1_gu, ffn1_down, mix_norm, ffn2_norm, ffn2_gu, ffn2_down,
                gdn_w_in, gdn_conv, gdn_a_log, gdn_dt_bias, gdn_out_norm, fox_w_in, w_out,
                mem_norm, mem_w_kv, kv_norm, kv_w, kv_b_f, final_norm, kv_spill, out, phases):
    first_unit, first_group, unit_words = unit_plan(phases)
    units = len(unit_words)

    gain_after = {"memtr0": G_MEM, "xtr0": G_FFN1, "down0": G_MIX, "wout0": G_FFN2, "down1": G_KV,
                  "kv0": G_FFN1 + KT, "down2": G_MIX + KT, "wout1": G_FFN2 + KT, "down3": G_FINAL}
    sums_before, feeds_before = {}, {}
    for name in phases:
        if name in gain_after:
            feeds_before[name] = len(feeds_before)
            if name != "kv0":
                sums_before[name] = len(sums_before)
    last_update = phases[-2]
    gain_after[last_update] = G_FINAL
    fed_by = {"up0": "xtr0", "gdnin0": "down0", "up1": "wout0", "kv0": "down1", "up2": "kv0",
              "foxin0": "down2", "up3": "wout1"}

    with ExitStack() as ctx:
        def sem(name):
            return ctx.enter_context(nc.semaphore(name))

        base = (nc.sbuf_base + 63) // 64 * 64
        space = nc.sbuf_usable_end - base - 64
        ctx.enter_context(nc.sbuf_tensor("arena", [P, space // 4], F32))
        cursor = [base]

        def words(shape):
            n = 1
            for s in shape[1:]:
                n *= s
            return (4 * n + 31) // 32 * 32

        def place(name, shape, dtype=F32, at=None):
            where = cursor[0] if at is None else at
            t = nc.alloc_sbuf_tensor_at(name, shape, dtype, offset=where)
            if at is None:
                cursor[0] += words(shape)
            assert where + words(shape) <= nc.sbuf_usable_end
            return t

        class Region:

            def __init__(self, start, size):
                self.next, self.end = start, start + size

            def put(self, name, shape, dtype=F32):
                t = place(name, shape, dtype, at=self.next)
                self.next += words(shape)
                assert self.next <= self.end, name
                return t

        h = place("h", [P, KT, SEQ])
        ident = place("ident", [P, P])
        ones = place("ones", [P, P])
        gains = place("gains", [P, GAINS])
        conv_w = place("conv_w", [P, CONV * 3 * HEADS])
        eps = place("eps", [P, 2])
        small = place("small", [P, 8])
        rstd = place("rstd", [P, SEQ])
        square_sum = place("square_sum", [P, SEQ])
        c_rows = place("c_rows", [P, SEQ])
        mem_k = place("mem_k", [P, DEPTH, MT, MEM_LEN])
        mem_v = place("mem_v", [P, DEPTH, MT, MEM_WIDTH])
        pair_at = cursor[0]
        PAIR_BYTES = 8224
        gate_up = place("gate_up", [P, 2, 2, SEQ])
        cursor[0] = pair_at + PAIR_BYTES
        raw = [place(f"raw{s}", [P, FULL_UNIT]) for s in range(2)]
        w_hi = [place(f"w_hi{s}", [P, FULL_UNIT], F32R) for s in range(2)]
        w_lo = [place(f"w_lo{s}", [P, FULL_UNIT], F32R) for s in range(2)]
        x_at, X_BYTES = cursor[0], 2 * KT * SEQ * 4
        x_hi = place("x_hi", [P, KT, SEQ], F32R)
        x_lo = place("x_lo", [P, KT, SEQ], F32R)
        h_at, H_BYTES = cursor[0], 2 * NP * SEQ * 4
        hid_hi = place("hid_hi", [P, NP, SEQ], F32R)
        hid_lo = place("hid_lo", [P, NP, SEQ], F32R)

        start = Region(h_at, H_BYTES)
        mem_tok = start.put("mem_tok", [P, MT, D_MODEL])
        x_tok = start.put("x_tok", [P, TT, D_MODEL])
        mem_t = start.put("mem_t", [P, KT, MEM_LEN])
        xm_hi = start.put("xm_hi", [P, KT, MEM_LEN], F32R)
        xm_lo = start.put("xm_lo", [P, KT, MEM_LEN], F32R)
        mem_vt = start.put("mem_vt", [P, DEPTH, MT, MEM_LEN])
        rstd_mem = start.put("rstd_mem", [P, MEM_LEN])
        gain_rows = start.put("gain_rows", [P, P])
        conv_rows = start.put("conv_rows", [P, P])

        mixer = Region(h_at, H_BYTES)
        q = mixer.put("q", [P, HEADS, SEQ])
        k = mixer.put("k", [P, HEADS, SEQ])
        v = mixer.put("v", [P, HEADS, SEQ])
        z = mixer.put("z", [P, HEADS, SEQ])
        q_mem = mixer.put("q_mem", [P, MT, SEQ])
        decay_beta = mixer.put("decay_beta", [P, HEADS, SEQ])
        decay = mixer.put("decay", [P, HEADS, SEQ])
        pick = mixer.put("pick", [P, HEADS, P])
        causal = mixer.put("causal", [P, P])
        level = mixer.put("level", [P, HEADS, P])
        tail = mixer.next
        gate_rows = place("gate_rows", [P, SEQ], at=tail)
        gate_cols = place("gate_cols", [P, TT, 4, 8], at=tail + 2048)
        a_row = place("a_row", [P, SEQ], at=tail + 2560)
        state0 = place("state0", [P, HEADS, P], at=tail + 2560)
        assert tail + 2560 + 3072 <= h_at + H_BYTES
        conv_in = place("conv_in", [P, 2, CONV - 1 + SEQ], at=pair_at)
        sq = [place(f"sq{o}", [P, SEQ], at=pair_at + 4128 + 2048 * o) for o in range(2)]
        restart = place("restart", [P, SEQ], at=pair_at + 4128 + 2048)

        core = Region(x_at, X_BYTES)
        inv = core.put("inv", [P, HEADS, P])
        inv_t = core.put("inv_t", [P, HEADS, P])
        below = [core.put(f"below{b}", [P, HEADS, P]) for b in range(2)]
        step_y = core.put("step_y", [P, HEADS, P])
        k_tail = core.put("k_tail", [P, HEADS, P])
        k_rhs = core.put("k_rhs", [P, HEADS, P])
        v_rhs = core.put("v_rhs", [P, HEADS, P])
        exp_g = core.put("exp_g", [P, HEADS, P])
        state1 = core.put("state1", [P, HEADS, P])
        state = [state0, state1]
        pair_region = Region(pair_at, PAIR_BYTES)
        v_new = pair_region.put("v_new", [P, HEADS, P])
        o_pair = pair_region.put("o_pair", [P, HEADS, P])
        o_sq, o_rms = k_rhs, v_rhs

        att = Region(x_at, X_BYTES)
        mp = [att.put(f"mp{b}", [P, TT, MEM_LEN]) for b in range(2)]
        mpt = att.put("mpt", [P, MT, SEQ])
        m_stat = att.put("m_stat", [P, 2, 4, TT])

        fox = Region(h_at, H_BYTES)
        fq = fox.put("fq", [P, HEADS, SEQ])
        fk = fox.put("fk", [P, HEADS, SEQ])
        fvt = fox.put("fvt", [P, HEADS, SEQ])
        fq_mem = fox.put("fq_mem", [P, MT, SEQ])
        fv = fox.put("fv", [P, TT, WIDTH])
        fpick = fox.put("fpick", [P, HEADS, P])
        bias_ts = [fox.put(f"bias_ts{b}", [P, SEQ]) for b in range(3)]
        fp = [fox.put(f"fp{b}", [P, SEQ]) for b in range(4)]
        fpt = [fox.put(f"fpt{b}", [P, SEQ]) for b in range(2)]
        c_cols = fox.put("c_cols", [P, TT, 8])
        f_stat = fox.put("f_stat", [P, 4, 4])
        f_x = place("f_x", [P, SEQ], at=h_at)
        f_t = place("f_t", [P, SEQ], at=h_at + 2048)
        f_one = place("f_one", [P, SEQ], at=h_at + 4096)
        kv_out = [place(f"kv_out{b}", [P, 2, SEQ], at=pair_at + 4096 * b) for b in range(2)]

        end = Region(x_at, X_BYTES)
        y_t = end.put("y_t", [P, KT, SEQ])
        y_tok = end.put("y_tok", [P, TT, D_MODEL])

        ps = ctx.enter_context(nc.psum_tensor("ps", [P, 8, SEQ], F32))

        CONSTS = 2
        MIXER_CONSTS, FOX_CONSTS = 28, 2

        releases = {"wout0": 0, "kv0": 1, "wout1": 2}
        N_REL = KT - 1
        SETS = (4, 6, 0, 2)

        def heads_of(b):
            return ps[:, b:b + 2, :].rearrange("p b n -> p (b n)")[:, 0:WIDTH].rearrange(
                "p (h n) -> p h n", h=HEADS)

        def pair_cols(p):
            return slice(p * P, (p + 1) * P)

        def over_columns(a, n):
            return a.rearrange("p (h o) -> p h o", o=1).broadcast_to([P, a.shape[1], n])

        def over_heads(a, n=HEADS):
            return a.rearrange("p (o n) -> p o n", o=1).broadcast_to([P, n, a.shape[1]])

        mem_in, gains_in, x_in, conv_in_sem, small_in = (sem(n) for n in (
            "mem_in", "gains_in", "x_in", "conv_w_in", "small_in"))
        consts = sem("consts")
        dve_consts = sem("dve_consts")
        table_tr, tables = sem("table_tr"), sem("tables")
        raw_in = [sem(f"raw_in{s}") for s in range(2)]
        hi_ready, lo_ready = sem("hi_ready"), sem("lo_ready")
        unit_done = sem("unit_done")
        turned = sem("turned")
        evac = sem("evac")
        sq_ready, sum_zero, sum_ready = sem("sq_ready"), sem("sum_zero"), sem("sum_ready")
        sum_done = sem("sum_done")
        rms_ready, rstd_ready = sem("rms_ready"), sem("rstd_ready")
        x_hi_ready, x_ready = sem("x_hi_ready"), sem("x_ready")
        x_free = sem("x_free")
        silu_ready, prod_ready = sem("silu_ready"), sem("prod_ready")
        hid_hi_ready, hid_ready = sem("hid_hi_ready"), sem("hid_ready")

        mix_hi, mix_ready = sem("mix_hi"), sem("mix_ready")
        tap_ready, tap_step, conv_ready, act_ready = (sem(n) for n in (
            "tap_ready", "tap_step", "conv_ready", "act_ready"))
        l2_sq, l2_sum, l2_rms, l2_inv, l2_done = (sem(n) for n in (
            "l2_sq", "l2_sum", "l2_rms", "l2_inv", "l2_done"))
        row_a, row_d, gate_turned, cols_ready = (sem(n) for n in (
            "row_a", "row_d", "gate_turned", "cols_ready"))
        g_spread, diff_step, diff_ready, decay_exp, decay_ready, decay_beta_ready = (sem(n) for n in (
            "g_spread", "diff_step", "diff_ready", "decay_exp", "decay_ready", "decay_beta_ready"))
        mixer_consts = sem("mixer_consts")
        ma_score, ma_max, ma_bias, ma_exp, ma_inv, ma_norm, ma_turned, ma_copied, ma_pv, ma_out = (
            sem(n) for n in ("ma_score", "ma_max", "ma_bias", "ma_exp", "ma_inv", "ma_norm",
                             "ma_turned", "ma_copied", "ma_pv", "ma_out"))
        gram, qk, k_turned, v_turned = (sem(n) for n in ("gram", "qk", "k_turned", "v_turned"))
        low_ready, qk_ready, k_tok_ready, v_tok_ready = (sem(n) for n in (
            "low_ready", "qk_ready", "k_tok_ready", "v_tok_ready"))
        below_step, below_ready, inv0_ready = sem("below_step"), sem("below_ready"), sem("inv0_ready")
        inv_turned, inv_ready = sem("inv_turned"), sem("inv_ready")
        y_prod, step_y_ready, z_prod, inv_t_ready = (sem(n) for n in (
            "y_prod", "step_y_ready", "z_prod", "inv_t_ready"))
        u_prod, w_prod, u_ready, w_ready = (sem(n) for n in ("u_prod", "w_prod", "u_ready", "w_ready"))
        pair_g, exp_g_ready, q_head_ready = sem("pair_g"), sem("exp_g_ready"), sem("q_head_ready")
        ws_prod, v_new_ready, state_prod, o_prod = (sem(n) for n in (
            "ws_prod", "v_new_ready", "state_prod", "o_prod"))
        state_zero, state_decayed, state_ready = sem("state_zero"), sem("state_decayed"), sem("state_ready")
        o_copied, o_sq_ready, o_sum, o_rms_ready, o_inv, o_scaled, o_done = (sem(n) for n in (
            "o_copied", "o_sq_ready", "o_sum", "o_rms_ready", "o_inv", "o_scaled", "o_done"))
        f_a, f_d = sem("f_a"), sem("f_d")
        fox_consts, c_turned, c_cols_ready, fv_turned, fv_ready = (sem(n) for n in (
            "fox_consts", "c_turned", "c_cols_ready", "fv_turned", "fv_ready"))
        fc_spread, fb_ready, fb_masked, f_score, f_biased, f_max, f_exp, f_inv, f_norm = (
            sem(n) for n in ("fc_spread", "fb_ready", "fb_masked", "f_score", "f_biased", "f_max",
                             "f_exp", "f_inv", "f_norm"))
        f_turned, f_copied, f_pv, f_out = (sem(n) for n in ("f_turned", "f_copied", "f_pv", "f_out"))
        y_gained, y_turned, y_moved = sem("y_gained"), sem("y_turned"), sem("y_moved")
        y_scale = sem("y_scale")
        y_ready, y_ready_odd, out_done = sem("y_ready"), sem("y_ready_odd"), sem("out_done")
        kv_ready, kv_spilled, kv_back = sem("kv_ready"), [sem(f"kv_spilled{b}") for b in range(2)], sem("kv_back")

        mem_rows = mem.rearrange("b (t p) d -> p (b t) d", p=P)
        x_rows = x.rearrange("b (t p) d -> p (b t) d", p=P)
        out_rows = out.rearrange("b (t p) d -> p (b t) d", p=P)

        def blocks(w):
            return w.rearrange("(k p) n -> p k n", p=P)

        ffn_gu = [blocks(w[l]) for l in range(DEPTH) for w in (ffn1_gu, ffn2_gu)]
        ffn_down = [blocks(w[l]) for l in range(DEPTH) for w in (ffn1_down, ffn2_down)]

        def slot(u0):
            return u0 % 2

        def weights_landed(u0, i=0):
            return 32 * (u0 // 2 + 1) + 32 * i

        block = ctx.enter_context(nc.Block())

        @block.sync
        def _(sp):
            def load(u0, parts, i=0):
                if u0 >= 2:
                    sp.wait_ge(lo_ready, u0 - 1 + 2 * i)
                for dst, src in parts:
                    sp.dma_start(dst, src).then_inc(raw_in[slot(u0)], 16)

            def load_cols(u0, w, col, i=0, width=2 * P):
                dst = raw[slot(u0)][:, 0:KT * width].rearrange("p (k n) -> p k n", k=KT)
                half = KT // 2
                load(u0, [(dst[:, a:a + half, :], w[:, a:a + half, bass.ds(col, width)])
                          for a in (0, half)], i)

            def load_gate_up(u0, w, n, i=0):
                dst = raw[slot(u0)][:].rearrange("p (k g n) -> p k g n", k=KT, g=2)
                load(u0, [(dst[:, :, g, :], w[:, :, bass.ds(g * FFN + n, P)]) for g in (0, 1)], i)

            def load_down(u0, w, half, n, i=0):
                dst = raw[slot(u0)][:, 0:DOWN_UNIT].rearrange("p (k n) -> p k n", k=HALF)
                cut = HALF // 2
                load(u0, [(dst[:, a:b, :], w[:, half * HALF + a:half * HALF + b, bass.ds(n, P)])
                          for a, b in ((0, cut), (cut, HALF))], i)

            for name in phases:
                kind, idx = name[:-1], int(name[-1])
                u = first_unit[name]
                if kind == "memtr":
                    sp.dma_start(mem_tok[:], mem_rows).then_inc(mem_in, 16)
                elif kind == "memkv":
                    for n in range(2):
                        load_cols(u + n, blocks(mem_w_kv[idx]), n * MEM_WIDTH)
                elif kind == "up":
                    for n in range(2):
                        load_gate_up(u + n, ffn_gu[idx], n * P)
                    with sp.Fori(0, NP // 2 - 1) as i:
                        for j in range(2):
                            load_gate_up(u + 2 + j, ffn_gu[idx], (2 * i + (2 + j)) * P, i)
                elif kind == "down":
                    with sp.Fori(0, KT) as m:
                        for half in range(2):
                            load_down(u + half, ffn_down[idx], half, m * P, m)
                elif kind == "gdnin":
                    w = blocks(gdn_w_in[0])
                    dst = raw[slot(u)][:, 0:KT * P].rearrange("p (k n) -> p k n", k=KT)
                    a_col = 4 * WIDTH
                    load(u, [(dst[:, :, 0:ROW_B], w[:, :, a_col:a_col + ROW_B]),
                             (dst[:, :, ROW_B:P], w[:, :, a_col + HEADS:a_col + HEADS + P - ROW_B])])
                    for n in range(12):
                        load_cols(u + 1 + n, w, n * 2 * P)
                    load_cols(u + 13, w, 4 * WIDTH + 2 * HEADS)
                elif kind == "foxin":
                    for n in range(4):
                        load_cols(u + n, blocks(fox_w_in[0]), n * 2 * P)
                elif kind == "wout":
                    for n in range(KT // 2):
                        load_cols(u + n, blocks(w_out[idx]), n * 2 * P)
                elif kind == "kv":
                    w = blocks(kv_w)
                    dst = raw[slot(u)][:, 0:KT * P].rearrange("p (k n) -> p k n", k=KT)
                    load(u, [(dst[:, :, 0:HEADS], w[:, :, 2 * WIDTH:2 * WIDTH + HEADS]),
                             (dst[:, :, HEADS:P], w[:, :, 0:P - HEADS])])
                    for n in range(HEADS):
                        load_cols(u + 1 + n, w, n * 2 * P)
                elif kind == "final":
                    for t in range(TT):
                        sp.wait_ge((y_ready, y_ready_odd)[t % 2], t // 2 + 1)
                        sp.dma_start(out_rows[:, t, :], y_tok[:, t, :]).then_inc(out_done, 16)
                    sp.wait_ge(out_done, 16 * TT)

        @block.tensor
        def _(pe):
            def bank_of(g0):
                return 2 * (g0 % 2)

            def bank_free(g0, i=0):
                if g0 >= 2:
                    pe.wait_ge(evac, g0 - 1 + 2 * i)

            def split_products(dst, hi, lo, xh, xl, first, last):
                nc.tensor.matmul(dst, hi, xh, start=first, stop=False)
                nc.tensor.matmul(dst, hi, xl, start=False, stop=False)
                return nc.tensor.matmul(dst, lo, xh, start=False, stop=last)

            def unit(u0, g0, xh, xl, i=0, outs=2, tokens=SEQ, feed=None, ready=x_ready, release=False):
                s, width = slot(u0), outs * P
                pe.wait_ge(lo_ready, u0 + 1 + 2 * i)
                bank_free(g0, i)
                for c in range(KT):
                    if feed is not None:
                        pe.wait_ge(ready, feed + c + 1)
                    for o in range(outs):
                        at = c * width + o * P
                        last = split_products(ps[:, bank_of(g0) + o, 0:tokens], w_hi[s][:, at:at + P],
                                              w_lo[s][:, at:at + P], xh[:, c, :], xl[:, c, :],
                                              c == 0, c == KT - 1)
                    if release and c < KT - 1:
                        last.then_inc(x_free, 1)
                last.then_inc(unit_done, 1)

            def down_tile(u0, g0, hid_wait=None, i=0):
                for half in range(2):
                    s = slot(u0 + half)
                    pe.wait_ge(lo_ready, u0 + half + 1 + 4 * i)
                    if half == 0:
                        bank_free(g0, i)
                    if hid_wait is not None:
                        pe.wait_ge(hid_ready, hid_wait + (half + 1) * HALF)
                    for c in range(HALF):
                        n = half * HALF + c
                        last = split_products(ps[:, bank_of(g0), :], w_hi[s][:, c * P:(c + 1) * P],
                                              w_lo[s][:, c * P:(c + 1) * P], hid_hi[:, n, :],
                                              hid_lo[:, n, :], n == 0, n == NP - 1)
                    last.then_inc(unit_done, 1)

            def spread_sum(name, tokens=SEQ):
                pe.wait_ge(sum_ready, KT * (sums_before[name] + 1))
                nc.tensor.matmul(ps[:, 4, 0:tokens], ones[:], square_sum[:, 0:tokens],
                                 start=True, stop=True).then_inc(sum_done, 1)

            def memory_attention(idx, qm):
                def scores(hd):
                    t, r0, n = hd // 2, MEM_HEAD * (hd % 2), MEM_HEADS * idx + hd
                    if hd:
                        pe.wait_ge(ma_exp, n)
                    for i in range(TT):
                        last = nc.tensor.matmul(
                            ps[:, 4 + i // 2, (i % 2) * MEM_LEN:(i % 2 + 1) * MEM_LEN],
                            qm[r0:r0 + MEM_HEAD, t, i * P:(i + 1) * P],
                            mem_k[r0:r0 + MEM_HEAD, idx, t, :], start=True, stop=True)
                    last.then_inc(ma_score, 1)

                scores(0)
                for hd in range(MEM_HEADS):
                    n, r0 = MEM_HEADS * idx + hd, MEM_HEAD * (hd % 2)
                    if hd + 1 < MEM_HEADS:
                        scores(hd + 1)
                    pe.wait_ge(ma_norm, n + 1)
                    if hd:
                        pe.wait_ge(ma_copied, n)
                    for st in range(MT):
                        for i in range(TT):
                            last = nc.tensor.transpose(ps[:, 6 + st, i * P:(i + 1) * P],
                                                       mp[hd % 2][:, i, st * P:(st + 1) * P], ident[:])
                    last.then_inc(ma_turned, 1)
                    pe.wait_ge(ma_copied, n + 1)
                    if hd >= 2:
                        pe.wait_ge(ma_out, n - 1)
                    for st in range(MT):
                        last = nc.tensor.matmul(ps[r0:r0 + MEM_HEAD, hd % 2, :],
                                                mem_v[:, idx, st, hd * MEM_HEAD:(hd + 1) * MEM_HEAD],
                                                mpt[:, st, :], start=st == 0, stop=st == MT - 1)
                    last.then_inc(ma_pv, 1)

            for name in phases:
                kind, idx = name[:-1], int(name[-1])
                u, g = first_unit[name], first_group[name]
                if kind == "memtr":
                    pe.wait_ge(consts, CONSTS)
                    pe.wait_ge(gains_in, 16 * 7)
                    nc.tensor.transpose(ps[:, 4, 0:GAINS], gain_rows[0:GAINS, :], ident[0:GAINS, 0:GAINS]).then_inc(table_tr, 1)
                    pe.wait_ge(conv_in_sem, 16)
                    nc.tensor.transpose(ps[:, 5, 0:4 * 18], conv_rows[0:72, :], ident[0:72, 0:72]).then_inc(table_tr, 1)
                    pe.wait_ge(mem_in, 16)
                    for c in range(KT):
                        bank_free(g + c)
                        for t in range(MT):
                            last = nc.tensor.transpose(ps[:, bank_of(g + c), t * P:(t + 1) * P],
                                                       mem_tok[:, t, c * P:(c + 1) * P], ident[:])
                        last.then_inc(turned, 1)
                elif kind == "memkv":
                    for n in range(2):
                        unit(u + n, g + n, xm_hi, xm_lo, tokens=MEM_LEN,
                             feed=0 if (idx, n) == (0, 0) else None)
                        if (idx, n) == (0, 0):
                            spread_sum("memtr0", MEM_LEN)
                elif kind == "memvtr":
                    for l in range(DEPTH):
                        pe.wait_ge(evac, g)
                        bank_free(g + l)
                        for t in range(MT):
                            for c in range(MT):
                                last = nc.tensor.transpose(
                                    ps[:, bank_of(g + l), (t * MT + c) * P:(t * MT + c + 1) * P],
                                    mem_vt[:, l, c, t * P:(t + 1) * P], ident[:])
                        last.then_inc(turned, 1)
                elif kind == "xtr":
                    for t in range(TT):
                        pe.wait_ge(x_in, 16 * TT)
                    for c in range(KT):
                        bank_free(g + c)
                        for t in range(TT):
                            last = nc.tensor.transpose(ps[:, bank_of(g + c), t * P:(t + 1) * P],
                                                       x_tok[:, t, c * P:(c + 1) * P], ident[:])
                        last.then_inc(turned, 1)
                elif kind == "up":
                    unit(u, g, x_hi, x_lo, feed=KT * feeds_before[fed_by[name]])
                    if fed_by[name] != "kv0":
                        spread_sum(fed_by[name])
                    unit(u + 1, g + 1, x_hi, x_lo)
                    with pe.Fori(0, NP // 2 - 1) as i:
                        for j in range(2):
                            unit(u + 2 + j, g + 2 + j, x_hi, x_lo, i)
                elif kind == "down":
                    down_tile(u, g, hid_wait=NP * idx)
                    down_tile(u + 2, g + 1)
                    with pe.Fori(0, KT // 2 - 1) as i:
                        for j in range(2):
                            down_tile(u + 4 + 2 * j, g + 2 + j, i=i)
                elif kind == "gdnin":
                    for n in range(14):
                        unit(u + n, g + n, x_hi, x_lo, outs=1 if n == 0 else 2,
                             feed=KT * feeds_before[fed_by[name]] if n == 0 else None)
                        if n == 0:
                            spread_sum(fed_by[name])
                        if 2 <= n <= 7:
                            pe.wait_ge(l2_sq, n - 1)
                            for o in range(2):
                                last = nc.tensor.matmul(ps[:, 6 + o, :], ones[:], sq[o][:],
                                                        start=True, stop=True)
                            last.then_inc(l2_sum, 1)
                        if n == 3:
                            pe.wait_ge(row_d, 8)
                            for t in range(TT):
                                last = nc.tensor.transpose(ps[:, 5, t * P:(t + 1) * P],
                                                           gate_rows[:, t * P:(t + 1) * P], ident[:])
                            last.then_inc(gate_turned, 1)
                        if 7 <= n <= 12:
                            hd = n - 7
                            pe.wait_ge(mixer_consts, MIXER_CONSTS)
                            if hd == 0:
                                pe.wait_ge(cols_ready, 1)
                            else:
                                pe.wait_ge(decay_beta_ready, hd)
                            nc.tensor.matmul(ps[:, 4, :], pick[0:HEADS, hd, :], gate_rows[0:HEADS, :],
                                             start=True, stop=True)
                            nc.tensor.matmul(ps[:, 5, :], pick[ROW_B:ROW_B + HEADS, hd, :],
                                             gate_rows[ROW_B:ROW_B + HEADS, :],
                                             start=True, stop=True).then_inc(g_spread, 1)
                elif kind == "gdn":
                    A, B, C, D = (heads_of(b) for b in SETS)
                    pe.wait_ge(evac, first_group["gdnin0"] + 14)
                    pe.wait_ge(decay_beta_ready, HEADS)
                    memory_attention(0, q_mem)
                    pe.wait_ge(ma_out, MEM_HEADS)
                    pe.wait_ge(l2_done, HEADS)
                    pe.wait_ge(act_ready, 9)

                    def each_head(dst, lhs, rhs, signal):
                        for hd in range(HEADS):
                            last = nc.tensor.matmul(dst[:, hd, :], lhs(hd), rhs(hd), start=True, stop=True)
                        last.then_inc(signal, 1)

                    def turn_heads(dst, src, signal):
                        for hd in range(HEADS):
                            last = nc.tensor.transpose(dst[:, hd, :], src(hd), ident[:])
                        last.then_inc(signal, 1)

                    def output_sum(p):
                        pe.wait_ge(o_sq_ready, p + 1)
                        flat = o_sq[:].rearrange("p h n -> p (h n)")
                        nc.tensor.matmul(ps[:, 2, :], ones[:], flat[:, 0:SEQ], start=True, stop=True)
                        nc.tensor.matmul(ps[:, 3, 0:WIDTH - SEQ], ones[:], flat[:, SEQ:WIDTH],
                                         start=True, stop=True).then_inc(o_sum, 1)

                    for p in range(TT):
                        cs = pair_cols(p)
                        if p:
                            pe.wait_ge(v_new_ready, 2 * p)
                        each_head(A, lambda hd: k[:, hd, cs], lambda hd: k[:, hd, cs], gram)
                        if p:
                            pe.wait_ge(state_ready, 2 * p)
                        turn_heads(C, lambda hd: k[:, hd, cs], k_turned)
                        if p:
                            output_sum(p - 1)
                            pe.wait_ge(o_copied, p)
                        each_head(B, lambda hd: k[:, hd, cs], lambda hd: q[:, hd, cs], qk)
                        if p:
                            pe.wait_ge(o_rms_ready, p)
                        turn_heads(D, lambda hd: v[:, hd, cs], v_turned)
                        pe.wait_ge(inv0_ready, p + 1)
                        pe.wait_ge(low_ready, p + 1)
                        turn_heads(A, lambda hd: inv_t[:, hd, :], inv_turned)
                        for lv in range(1, HEADS):
                            n = 5 * p + lv
                            pe.wait_ge(inv_ready, n)
                            pe.wait_ge(below_ready, n)
                            each_head(A, lambda hd: below[lv % 2][:, hd, :], lambda hd: inv[:, hd, :], y_prod)
                            pe.wait_ge(step_y_ready, n)
                            if lv == 1:
                                pe.wait_ge(qk_ready, p + 1)
                            each_head(B, lambda hd: step_y[:, hd, :], lambda hd: inv_t[:, hd, :], z_prod)
                            if lv == 1:
                                pe.wait_ge(v_tok_ready, p + 1)
                                each_head(D, lambda hd: pick[0:HEADS, hd, :],
                                          lambda hd: gate_rows[0:HEADS, cs], pair_g)
                            pe.wait_ge(inv_t_ready, n)
                            if lv < 5:
                                turn_heads(A, lambda hd: inv_t[:, hd, :], inv_turned)
                        each_head(A, lambda hd: inv_t[:, hd, :], lambda hd: v_rhs[:, hd, :], u_prod)
                        pe.wait_ge(k_tok_ready, p + 1)
                        each_head(B, lambda hd: k_rhs[:, hd, :], lambda hd: inv_t[:, hd, :], w_prod)
                        pe.wait_ge(u_ready, p + 1)
                        pe.wait_ge(w_ready, p + 1)
                        pe.wait_ge(q_head_ready, p + 1)
                        for c in range(2):
                            n, r0 = 2 * p + c, CHUNK * c
                            rows, tok = slice(r0, r0 + CHUNK), slice(p * P + r0, p * P + r0 + CHUNK)
                            st = state[n % 2]
                            if n:
                                pe.wait_ge(state_ready, n)
                            else:
                                pe.wait_ge(state_zero, 1)
                            for hd in range(HEADS):
                                last = nc.tensor.matmul(A[rows, hd, :], k[:, hd, tok], st[:, hd, :],
                                                        start=True, stop=True)
                            last.then_inc(ws_prod, 1)
                            pe.wait_ge(v_new_ready, n + 1)
                            for hd in range(HEADS):
                                last = nc.tensor.matmul(C[:, hd, :], k_tail[rows, hd, :], v_new[rows, hd, :],
                                                        start=True, stop=True)
                            last.then_inc(state_prod, 1)
                            for hd in range(HEADS):
                                dst = B[:, hd, rows]
                                nc.tensor.matmul(dst, st[:, hd, :], q[:, hd, tok], start=True, stop=False)
                                last = nc.tensor.matmul(dst, v_new[rows, hd, :], decay[rows, hd, tok],
                                                        start=False, stop=True)
                            last.then_inc(o_prod, 1)
                    output_sum(TT - 1)
                elif kind == "wout":
                    for n in range(KT // 2):
                        unit(u + n, g + n, x_hi, x_lo, feed=KT * idx if n == 0 else None,
                             ready=mix_ready, release=n == KT // 2 - 1)
                elif kind == "kv":
                    for n in range(1 + HEADS):
                        unit(u + n, g + n, x_hi, x_lo, outs=1 if n == 0 else 2,
                             feed=KT * feeds_before[fed_by[name]] if n == 0 else None,
                             release=n == HEADS)
                        if n == 0:
                            spread_sum(fed_by[name])
                elif kind == "foxin":
                    for n in range(4):
                        unit(u + n, g + n, x_hi, x_lo,
                             feed=KT * feeds_before[fed_by[name]] if n == 0 else None)
                        if n == 0:
                            spread_sum(fed_by[name])
                elif kind == "fox":
                    pe.wait_ge(rms_ready, sums_before["down2"] + 1)
                    for t in range(TT):
                        last = nc.tensor.transpose(ps[:, 4, t * 8:t * 8 + HEADS],
                                                   c_rows[0:HEADS, t * P:(t + 1) * P], ident[0:HEADS, 0:HEADS])
                    last.then_inc(c_turned, 1)
                    pe.wait_ge(kv_back, 32)
                    for hd in range(HEADS):
                        if hd >= 2:
                            pe.wait_ge(fv_ready, hd - 1)
                        for t in range(TT):
                            last = nc.tensor.transpose(ps[:, 6 + hd % 2, t * P:(t + 1) * P],
                                                       fvt[:, hd, t * P:(t + 1) * P], ident[:])
                        last.then_inc(fv_turned, 1)
                    pe.wait_ge(fv_ready, HEADS)
                    pe.wait_ge(c_cols_ready, 1)
                    pe.wait_ge(evac, first_group["foxin0"] + 4)
                    memory_attention(1, fq_mem)
                    pe.wait_ge(ma_out, 2 * MEM_HEADS)
                    pe.wait_ge(fox_consts, FOX_CONSTS)

                    def spread_c(hd):
                        if hd >= 2:
                            pe.wait_ge(fb_ready, TT * (hd - 1))
                        nc.tensor.matmul(ps[:, hd % 2, :], fpick[0:HEADS, hd, :], c_rows[0:HEADS, :],
                                         start=True, stop=True).then_inc(fc_spread, 1)

                    spread_c(0)
                    for n in range(HEADS * TT + 2):
                        if n < HEADS * TT:
                            hd, i = divmod(n, TT)
                            if n % TT == 2 and hd + 1 < HEADS:
                                spread_c(hd + 1)
                            if n >= 2:
                                pe.wait_ge(f_biased, n - 1)
                            nc.tensor.matmul(ps[:, 4 + n % 2, 0:(i + 1) * P], fq[:, hd, i * P:(i + 1) * P],
                                             fk[:, hd, 0:(i + 1) * P], start=True, stop=True).then_inc(f_score, 1)
                        if n >= 2:
                            m = n - 2
                            hd, i = divmod(m, TT)
                            pe.wait_ge(f_norm, m + 1)
                            if m >= 2:
                                pe.wait_ge(f_copied, m - 1)
                            for s in range(i + 1):
                                last = nc.tensor.transpose(ps[:, 6 + m % 2, s * P:(s + 1) * P],
                                                           fp[m % 4][:, s * P:(s + 1) * P], ident[:])
                            last.then_inc(f_turned, 1)
                            pe.wait_ge(f_copied, m + 1)
                            if i == 0 and hd >= 2:
                                pe.wait_ge(f_out, hd - 1)
                            for s in range(i + 1):
                                last = nc.tensor.matmul(ps[:, 2 + hd % 2, i * P:(i + 1) * P],
                                                        fv[:, s, hd * P:(hd + 1) * P],
                                                        fpt[m % 2][:, s * P:(s + 1) * P],
                                                        start=s == 0, stop=s == i)
                            last.then_inc(f_pv, 1)
                elif kind == "final":
                    for c in range(KT):
                        pe.wait_ge(y_gained, c + 1)
                        if c >= 2:
                            pe.wait_ge(y_moved, c - 1)
                        for t in range(TT):
                            last = nc.tensor.transpose(ps[:, 6 + c % 2, t * P:(t + 1) * P],
                                                       y_t[:, c, t * P:(t + 1) * P], ident[:])
                        last.then_inc(y_turned, 1)
                    pe.wait_ge(sum_ready, KT * (sums_before[last_update] + 1))
                    for t in range(TT):
                        last = nc.tensor.matmul(ps[:, 4, t:t + 1], square_sum[:, t * P:(t + 1) * P],
                                                ones[:, 0:1], start=True, stop=True)
                    last.then_inc(sum_done, 1)

        @block.scalar
        def _(act):
            def round_hi(u, i=0):
                if not isinstance(u, int) or u < units:
                    n, s = unit_words[u], slot(u)
                    act.wait_ge(raw_in[s], weights_landed(u, i))
                    if u >= 2:
                        act.wait_ge(unit_done, u - 1 + 2 * i)
                    nc.scalar.activation(w_hi[s][:, 0:n], raw[s][:, 0:n], ACT.Copy).then_inc(hi_ready, 1)

            def feed_hi(dst, src, gain):
                nc.scalar.activation(dst, src, ACT.Copy, scale=gain).then_inc(x_hi_ready, 1)

            def square_free(name, c, i=0):
                done = KT * sums_before[name] + c
                if done >= 2:
                    act.wait_ge(sum_ready, done - 1 + 2 * i)

            def square(name, b, c, src, tokens=SEQ, looped=False):
                if not looped:
                    square_free(name, c)
                nc.scalar.activation(gate_up[:, b, 0, 0:tokens], src, ACT.Square).then_inc(sq_ready, 1)

            def root_mean_square(name, dst, tokens=SEQ):
                act.wait_ge(sum_done, sums_before[name] + 1)
                nc.scalar.activation(dst, ps[:, 4, 0:tokens], ACT.Sqrt, scale=1.0 / D_MODEL,
                                     bias=eps[:, 0:1]).then_inc(rms_ready, 1)

            def memory_attention(idx):
                if idx == 0:
                    act.wait_ge(evac, first_group["gdnin0"] + 14)
                for hd in range(MEM_HEADS):
                    n, b = MEM_HEADS * idx + hd, hd % 2
                    act.wait_ge(ma_bias, n + 1)
                    for i in range(TT):
                        last = nc.scalar.activation(
                            mp[b][:, i, :], ps[:, 4 + i // 2, (i % 2) * MEM_LEN:(i % 2 + 1) * MEM_LEN],
                            ACT.Exp, scale=MEM_HEAD ** -0.5, bias=m_stat[:, b, 1, i:i + 1],
                            accum_out=m_stat[:, b, 2, i:i + 1])
                    last.then_inc(ma_exp, 1)

            for name in phases:
                kind, idx = name[:-1], int(name[-1])
                u, g = first_unit[name], first_group[name]
                gain = gain_after.get(name)
                if kind == "memtr":
                    row = 0
                    for vec in (ffn1_norm, mix_norm, ffn2_norm, kv_norm, final_norm, mem_norm, gdn_out_norm):
                        flat = vec if len(vec.shape) == 1 else vec.rearrange("a b -> (a b)")
                        n = flat.shape[0] // P
                        act.dma_start(gain_rows[row:row + n, :], flat.rearrange("(r c) -> r c", c=P)).then_inc(gains_in, 16)
                        row += n
                    act.dma_start(conv_rows[0:4 * 18, :], gdn_conv.rearrange("o j (r c) -> (o j r) c", c=P)).then_inc(conv_in_sem, 16)
                    for t in range(TT):
                        act.dma_start(x_tok[:, t, :], x_rows[:, t, :]).then_inc(x_in, 16)
                    act.dma_start(small[0:HEADS, 0:1], gdn_a_log.rearrange("o h -> h o")).then_inc(small_in, 16)
                    act.dma_start(small[0:HEADS, 1:2], gdn_dt_bias.rearrange("o h -> h o")).then_inc(small_in, 16)
                    act.dma_start(small[0:HEADS, 2:3], kv_b_f.rearrange("(h o) -> h o", o=1)).then_inc(small_in, 16)
                    round_hi(0)
                    round_hi(1)
                    act.wait_ge(small_in, 48)
                    act.wait_ge(tables, 2)
                    for c in range(KT):
                        act.wait_ge(evac, g + c + 1)
                        feed_hi(xm_hi[:, c, :], mem_t[:, c, :], gains[:, gain + c:gain + c + 1])
                        square(name, c % 2, c, mem_t[:, c, :], MEM_LEN)
                elif kind == "memkv":
                    for n in range(2):
                        if (idx, n) == (0, 0):
                            act.wait_ge(dve_consts, 2)
                            root_mean_square("memtr0", rstd_mem[:], MEM_LEN)
                        round_hi(u + n + 2)
                elif kind == "xtr":
                    for c in range(KT):
                        act.wait_ge(evac, g + c + 1)
                        feed_hi(x_hi[:, c, :], h[:, c, :], gains[:, gain + c:gain + c + 1])
                        square(name, c % 2, c, h[:, c, :])
                elif kind == "up":
                    if fed_by[name] != "kv0":
                        root_mean_square(fed_by[name], rstd[:])

                    def step(n, j, i=0):
                        round_hi(u + n + 2, i)
                        act.wait_ge(evac, g + n + 1 + 2 * i)
                        nc.scalar.activation(gate_up[:, j, 0, :], gate_up[:, j, 0, :],
                                             ACT.Silu).then_inc(silu_ready, 1)
                        act.wait_ge(prod_ready, NP * idx + n + 1 + 2 * i)
                        at = n + 2 * i
                        nc.scalar.activation(hid_hi[:, bass.ds(at, 1), :], gate_up[:, j, 0:1, :],
                                             ACT.Copy).then_inc(hid_hi_ready, 1)

                    with act.Fori(0, NP // 2 - 1) as i:
                        for j in range(2):
                            step(j, j, i)
                    for j in range(2):
                        step(NP - 2 + j, j)
                elif kind == "down":
                    def step(m, j, i=0):
                        for half in range(2):
                            round_hi_4(u + 2 * m + half + 2, i)
                        square_free(name, m, i)
                        act.wait_ge(evac, g + m + 1 + 2 * i)
                        c = m + 2 * i
                        act.wait_ge(tables, 2)
                        if name != last_update:
                            feed_hi(x_hi[:, bass.ds(c, 1), :], h[:, bass.ds(c, 1), :],
                                    gains[:, bass.ds(gain + c, 1)])
                        square(name, j, m, h[:, bass.ds(c, 1), :].rearrange("p a n -> p (a n)"), looped=True)

                    def round_hi_4(w, i):
                        round_hi(w, 2 * i)

                    with act.Fori(0, KT // 2 - 1) as i:
                        for j in range(2):
                            step(j, j, i)
                    for j in range(2):
                        step(KT - 2 + j, j)
                elif kind == "gdnin":
                    qkv = [t[:, 2 * n:2 * n + 2, :] for t in (q, k, v) for n in range(HEADS // 2)]

                    for n in range(14):
                        if n == 0:
                            root_mean_square(fed_by[name], rstd[:])
                            round_hi(u + 2)
                            a, t = a_row[0:HEADS, :], c_rows[0:HEADS, :]
                            b = a_row[ROW_B:ROW_B + HEADS, :]
                            act.wait_ge(row_d, 1)
                            nc.scalar.activation(t, a, ACT.Abs).then_inc(row_a, 1)
                            act.wait_ge(row_a, 1)
                            nc.scalar.activation(t, t, ACT.Exp, scale=-1.0).then_inc(row_a, 1)
                            nc.scalar.activation(b, b, ACT.Exp, scale=-1.0).then_inc(row_a, 1)
                            nc.scalar.activation(small[0:HEADS, 3:4], small[0:HEADS, 0:1],
                                                 ACT.Exp).then_inc(row_a, 1)
                            act.wait_ge(row_a, 2)
                            nc.scalar.activation(t, t, ACT.Ln, bias=ones[0:HEADS, 0:1]).then_inc(row_a, 1)
                            act.wait_ge(row_d, 7)
                            nc.scalar.activation(c_rows[ROW_B:ROW_B + HEADS, :], gate_rows[0:HEADS, :],
                                                 ACT.Exp).then_inc(row_a, 1)
                            nc.scalar.activation(gate_rows[3 * ROW_B:3 * ROW_B + HEADS, :], a,
                                                 ACT.Exp).then_inc(row_a, 1)
                        elif n <= 9:
                            act.wait_ge(evac, g + n + 1)
                            for o in range(2):
                                tile = 2 * (n - 1) + o
                                last = nc.scalar.activation(
                                    qkv[n - 1][:, o, :], conv_in[:, o, CONV - 1:], ACT.Copy,
                                    scale=conv_w[:, 3 * 3 * HEADS + tile:3 * 3 * HEADS + tile + 1])
                            last.then_inc(tap_ready, 1)
                            round_hi(u + n + 2)
                            if 2 <= n <= 7:
                                act.wait_ge(l2_sum, n - 1)
                                query = n - 1 <= HEADS // 2
                                for o in range(2):
                                    last = nc.scalar.activation(
                                        sq[o][:], ps[:, 6 + o, :], ACT.Sqrt,
                                        scale=float(HEAD) if query else 1.0,
                                        bias=eps[:, 1:2] if query else eps[:, 0:1])
                                last.then_inc(l2_rms, 1)
                            act.wait_ge(conv_ready, n)
                            nc.scalar.activation(qkv[n - 1], qkv[n - 1], ACT.Silu).then_inc(act_ready, 1)
                        else:
                            round_hi(u + n + 2)
                            act.wait_ge(evac, g + n + 1)
                            if n <= 12:
                                zt = z[:, 2 * (n - 10):2 * (n - 10) + 2, :]
                                nc.scalar.activation(zt, zt, ACT.Silu).then_inc(act_ready, 1)
                        if 7 <= n <= 12:
                            hd = n - 7
                            act.wait_ge(diff_ready, hd + 1)
                            nc.scalar.activation(decay[:, hd, :], decay[:, hd, :], ACT.Exp).then_inc(decay_exp, 1)
                elif kind == "gdn":
                    memory_attention(0)
                    A, B, C, D = (heads_of(b) for b in SETS)
                    for p in range(TT):
                        cs = pair_cols(p)
                        for lv in range(1, HEADS):
                            n = 5 * p + lv
                            act.wait_ge(inv_turned, n)
                            if n > 1:
                                act.wait_ge(y_prod, n - 1)
                            nc.scalar.activation(inv[:], A, ACT.Copy).then_inc(inv_ready, 1)
                            act.wait_ge(y_prod, n)
                            if n > 1:
                                act.wait_ge(z_prod, n - 1)
                            nc.scalar.activation(step_y[:], A, ACT.Copy).then_inc(step_y_ready, 1)
                            if lv == 1:
                                act.wait_ge(pair_g, p + 1)
                                if p:
                                    act.wait_ge(state_decayed, 2 * p)
                                nc.scalar.activation(exp_g[:], D, ACT.Exp).then_inc(exp_g_ready, 1)
                        act.wait_ge(u_prod, p + 1)
                        nc.scalar.activation(v[:, :, cs], A, ACT.Copy).then_inc(u_ready, 1)
                        act.wait_ge(o_prod, 2 * (p + 1))
                        nc.scalar.activation(o_pair[:], B, ACT.Copy).then_inc(o_copied, 1)
                        act.wait_ge(o_copied, p + 1)
                        nc.scalar.activation(o_sq[:], o_pair[:], ACT.Square).then_inc(o_sq_ready, 1)
                        act.wait_ge(o_sum, p + 1)
                        nc.scalar.activation(o_rms[:], D, ACT.Sqrt, scale=1.0 / HEAD,
                                             bias=eps[:, 0:1]).then_inc(o_rms_ready, 1)
                elif kind == "wout":
                    qs, qm = (q, q_mem) if idx == 0 else (fq, fq_mem)
                    if idx == 0:
                        act.wait_ge(o_done, TT)
                    else:
                        act.wait_ge(f_out, HEADS)
                    for c in range(KT):
                        src = qs[:, c, :] if c < HEADS else qm[:, c - HEADS, :]
                        nc.scalar.activation(x_hi[:, c, :], src, ACT.Copy).then_inc(mix_hi, 1)
                    for n in range(KT // 2):
                        act.wait_ge(evac, g + n + 1)
                        if n == KT // 2 - 1:
                            for c in (KT - 2, KT - 1):
                                if c == KT - 2:
                                    act.wait_ge(x_free, N_REL * (releases[name] + 1))
                                feed_hi(x_hi[:, c, :], h[:, c, :], gains[:, gain + c:gain + c + 1])
                        for c in (2 * n, 2 * n + 1):
                            square(name, c % 2, c, h[:, c, :])
                        round_hi(u + n + 2)
                        if n == KT // 2 - 2:
                            for c in range(KT - 2):
                                act.wait_ge(x_free, N_REL * releases[name] + c + 1)
                                feed_hi(x_hi[:, c, :], h[:, c, :], gains[:, gain + c:gain + c + 1])
                elif kind == "kv":
                    root_mean_square(fed_by[name], rstd[:])
                    for n in range(1 + HEADS):
                        if n == HEADS:
                            act.wait_ge(unit_done, u + n + 1)
                            c = KT - 1
                            feed_hi(x_hi[:, c, :], h[:, c, :], gains[:, gain + c:gain + c + 1])
                        round_hi(u + n + 2)
                        if n == 0:
                            t = f_t[0:HEADS, :]
                            act.wait_ge(f_d, 1)
                            nc.scalar.activation(t, f_x[0:HEADS, :], ACT.Abs).then_inc(f_a, 1)
                            act.wait_ge(f_a, 1)
                            nc.scalar.activation(t, t, ACT.Exp, scale=-1.0).then_inc(f_a, 1)
                            act.wait_ge(f_a, 2)
                            nc.scalar.activation(t, t, ACT.Ln, bias=ones[0:HEADS, 0:1]).then_inc(f_a, 1)
                        if n == HEADS - 1:
                            for c in range(KT - 1):
                                act.wait_ge(x_free, N_REL * releases[name] + c + 1)
                                feed_hi(x_hi[:, c, :], h[:, c, :], gains[:, gain + c:gain + c + 1])
                elif kind == "foxin":
                    root_mean_square(fed_by[name], rstd[:])
                    for b in range(2):
                        act.wait_ge(kv_spilled[b], 16 * (HEADS // 2))
                    act.dma_start(fk[:], kv_spill[:, 0:HEADS, :]).then_inc(kv_back, 16)
                    act.dma_start(fvt[:], kv_spill[:, HEADS:2 * HEADS, :]).then_inc(kv_back, 16)
                    for n in range(4):
                        act.wait_ge(evac, g + n + 1)
                        round_hi(u + n + 2)
                elif kind == "fox":
                    memory_attention(1)

                    def bias_of(n):
                        hd, i = divmod(n, TT)
                        if i == 0:
                            act.wait_ge(fc_spread, hd + 1)
                        if n >= 3:
                            act.wait_ge(f_biased, n - 2)
                        nc.scalar.activation(bias_ts[n % 3][:, 0:(i + 1) * P], ps[:, hd % 2, 0:(i + 1) * P],
                                             ACT.Identity, scale=-1.0,
                                             bias=c_cols[:, i, hd:hd + 1]).then_inc(fb_ready, 1)

                    bias_of(0)
                    bias_of(1)
                    for n in range(HEADS * TT + 2):
                        if n < HEADS * TT:
                            i = n % TT
                            act.wait_ge(f_max, n + 1)
                            nc.scalar.activation(fp[n % 4][:, 0:(i + 1) * P], fp[n % 4][:, 0:(i + 1) * P],
                                                 ACT.Exp, bias=f_stat[:, n % 4, 0:1],
                                                 accum_out=f_stat[:, n % 4, 1:2]).then_inc(f_exp, 1)
                        if n + 2 < HEADS * TT:
                            bias_of(n + 2)
                        if n >= 2:
                            m = n - 2
                            i = m % TT
                            act.wait_ge(f_turned, m + 1)
                            if m >= 2:
                                act.wait_ge(f_pv, m - 1)
                            nc.scalar.activation(fpt[m % 2][:, 0:(i + 1) * P], ps[:, 6 + m % 2, 0:(i + 1) * P],
                                                 ACT.Copy).then_inc(f_copied, 1)
                elif kind == "final":
                    root_mean_square(last_update, small[:, 4:8], TT)
                    for t in (1, 3):
                        act.wait_ge(y_moved, KT)
                        act.wait_ge(y_scale, 1)
                        nc.scalar.activation(y_tok[:, t, :], y_tok[:, t, :], ACT.Copy,
                                             scale=small[:, 4 + t:5 + t]).then_inc(y_ready_odd, 1)

        @block.vector
        def _(dve):
            def cut_lo(u, i=0):
                if u < units:
                    n, s = unit_words[u], slot(u)
                    dve.wait_ge(hi_ready, u + 1 + 2 * i)
                    nc.vector.tensor_tensor(w_lo[s][:, 0:n], raw[s][:, 0:n],
                                            w_hi[s][:, 0:n].bitcast(F32), ALU.subtract).then_inc(lo_ready, 1)

            def feed_lo(name, dst, src, gain, hi, c, i=0):
                dve.wait_ge(x_hi_ready, KT * feeds_before[name] + c + 1 + 2 * i)
                nc.vector.scalar_tensor_tensor(dst, src, gain, hi.bitcast(F32), op0=ALU.mult,
                                               op1=ALU.subtract).then_inc(x_ready, 1)

            def bank_of(g0):
                return 2 * (g0 % 2)

            def output_scale(p):
                dve.wait_ge(o_rms_ready, p + 1)
                nc.vector.reciprocal(o_rms[:], o_rms[:]).then_inc(o_inv, 1)
                dve.wait_ge(o_inv, p + 1)
                nc.vector.scalar_tensor_tensor(o_pair[:], o_pair[:], gains[:, G_OUT:G_OUT + 1], o_rms[:],
                                               op0=ALU.mult, op1=ALU.mult).then_inc(o_scaled, 1)

            def reciprocal_of_rms(name, dst):
                n = sums_before[name] + 1
                dve.wait_ge(rms_ready, n)
                nc.vector.reciprocal(dst, dst).then_inc(rstd_ready, 1)
                dve.wait_ge(rstd_ready, n)

            def scaled(dst, g0, outs, scale, tokens=SEQ, signal=None):
                src = ps[:, bank_of(g0):bank_of(g0) + outs, 0:tokens]
                by = scale.rearrange("p (o n) -> p o n", o=1).broadcast_to([P, outs, tokens])
                nc.vector.tensor_tensor(dst, src, by, ALU.mult).then_inc(evac, 1)

            nc.vector.memset(ones[:], 1.0).then_inc(dve_consts, 1)
            nc.vector.memset(eps[:, 0:1], EPS)
            nc.vector.memset(eps[:, 1:2], EPS * HEAD).then_inc(dve_consts, 1)

            def memory_attention(idx, qm):
                def negative_max(hd):
                    n, b = MEM_HEADS * idx + hd, hd % 2
                    dve.wait_ge(ma_score, n + 1)
                    src = ps[:, 4:6, :].rearrange("p b (i m) -> p (b i) m", i=2)
                    nc.vector.tensor_reduce(m_stat[:, b, 0, :], src, AX_X, ALU.max,
                                            negate=True).then_inc(ma_max, 1)
                    dve.wait_ge(ma_max, n + 1)
                    nc.vector.tensor_scalar(m_stat[:, b, 1, :], m_stat[:, b, 0, :], MEM_HEAD ** -0.5, None,
                                            op0=ALU.mult).then_inc(ma_bias, 1)

                negative_max(0)
                for hd in range(MEM_HEADS):
                    n, b, r0 = MEM_HEADS * idx + hd, hd % 2, MEM_HEAD * (hd % 2)
                    dve.wait_ge(ma_exp, n + 1)
                    nc.vector.reciprocal(m_stat[:, b, 3, :], m_stat[:, b, 2, :]).then_inc(ma_inv, 1)
                    dve.wait_ge(ma_inv, n + 1)
                    nc.vector.tensor_tensor(mp[b][:], mp[b][:], over_columns(m_stat[:, b, 3, :], MEM_LEN),
                                            ALU.mult).then_inc(ma_norm, 1)
                    if hd + 1 < MEM_HEADS:
                        negative_max(hd + 1)
                    dve.wait_ge(ma_turned, n + 1)
                    if hd:
                        dve.wait_ge(ma_pv, n)
                    nc.vector.tensor_copy(mpt[:], ps[:, 6:8, :]).then_inc(ma_copied, 1)
                    dve.wait_ge(ma_pv, n + 1)
                    nc.vector.tensor_copy(qm[r0:r0 + MEM_HEAD, hd // 2, :],
                                          ps[r0:r0 + MEM_HEAD, hd % 2, :]).then_inc(ma_out, 1)

            for name in phases:
                kind, idx = name[:-1], int(name[-1])
                u, g = first_unit[name], first_group[name]
                gain = gain_after.get(name)
                if kind == "memtr":
                    dve.wait_ge(table_tr, 1)
                    nc.vector.tensor_copy(gains[:], ps[:, 4, 0:GAINS]).then_inc(tables, 1)
                    dve.wait_ge(table_tr, 2)
                    nc.vector.tensor_copy(conv_w[:], ps[:, 5, 0:4 * 18]).then_inc(tables, 1)
                    dve.wait_ge(tables, 2)
                    for c in range(KT):
                        dve.wait_ge(turned, c + 1)
                        nc.vector.tensor_copy(mem_t[:, c, :], ps[:, bank_of(g + c), 0:MEM_LEN]).then_inc(evac, 1)
                        if c == 0:
                            cut_lo(0)
                            cut_lo(1)
                        if c >= 1:
                            feed_lo(name, xm_lo[:, c - 1, :], mem_t[:, c - 1, :],
                                    gains[:, gain + c - 1:gain + c], xm_hi[:, c - 1, :], c - 1)
                    c = KT - 1
                    feed_lo(name, xm_lo[:, c, :], mem_t[:, c, :], gains[:, gain + c:gain + c + 1],
                            xm_hi[:, c, :], c)
                elif kind == "memkv":
                    for n in range(2):
                        if (idx, n) == (0, 0):
                            reciprocal_of_rms("memtr0", rstd_mem[:])
                        dve.wait_ge(unit_done, u + n + 1)
                        dst = mem_k[:, idx] if n == 0 else mem_vt[:, idx]
                        scaled(dst, g + n, 2, rstd_mem[:], MEM_LEN)
                        cut_lo(u + n + 2)
                elif kind == "memvtr":
                    for l in range(DEPTH):
                        dve.wait_ge(turned, KT + l + 1)
                        nc.vector.tensor_copy(mem_v[:, l].rearrange("p t n -> p (t n)"),
                                              ps[:, bank_of(g + l), :]).then_inc(evac, 1)
                elif kind == "xtr":
                    for c in range(KT + 1):
                        if c < KT:
                            dve.wait_ge(turned, KT + DEPTH + c + 1)
                            nc.vector.tensor_copy(h[:, c, :], ps[:, bank_of(g + c), :]).then_inc(evac, 1)
                        if c >= 1:
                            feed_lo(name, x_lo[:, c - 1, :], h[:, c - 1, :],
                                    gains[:, gain + c - 1:gain + c], x_hi[:, c - 1, :], c - 1)
                elif kind == "up":
                    if fed_by[name] != "kv0":
                        reciprocal_of_rms(fed_by[name], rstd[:])
                    else:
                        for b in range(2):
                            dve.wait_ge(kv_spilled[b], 16 * (HEADS // 2))

                    def step(n, j, i=0):
                        dve.wait_ge(unit_done, u + n + 1 + 2 * i)
                        scaled(gate_up[:, j], g + n, 2, rstd[:])
                        cut_lo(u + n + 2, i)
                        dve.wait_ge(hid_hi_ready, NP * idx + n + 1 + 2 * i)
                        at = n + 2 * i
                        nc.vector.tensor_tensor(hid_lo[:, bass.ds(at, 1), :], gate_up[:, j, 0:1, :],
                                                hid_hi[:, bass.ds(at, 1), :].bitcast(F32),
                                                ALU.subtract).then_inc(hid_ready, 1)

                    with dve.Fori(0, NP // 2 - 1) as i:
                        for j in range(2):
                            step(j, j, i)
                    for j in range(2):
                        step(NP - 2 + j, j)
                elif kind == "down":
                    def step(m, j, i=0):
                        dve.wait_ge(unit_done, u + 2 * m + 1 + 4 * i)
                        cut_lo(u + 2 * m + 2, 2 * i)
                        dve.wait_ge(unit_done, u + 2 * m + 2 + 4 * i)
                        c = m + 2 * i
                        nc.vector.scalar_tensor_tensor(
                            h[:, bass.ds(c, 1), :], ps[:, bank_of(g + m):bank_of(g + m) + 1, :], 0.5,
                            h[:, bass.ds(c, 1), :], op0=ALU.mult, op1=ALU.add).then_inc(evac, 1)
                        if name != last_update:
                            feed_lo(name, x_lo[:, bass.ds(c, 1), :], h[:, bass.ds(c, 1), :],
                                    gains[:, bass.ds(gain + c, 1)], x_hi[:, bass.ds(c, 1), :], m, i)
                        else:
                            dve.wait_ge(evac, g + m + 1 + 2 * i)
                            nc.vector.tensor_scalar(y_t[:, bass.ds(c, 1), :], h[:, bass.ds(c, 1), :],
                                                    gains[:, bass.ds(gain + c, 1)], None,
                                                    op0=ALU.mult).then_inc(y_gained, 1)
                        cut_lo(u + 2 * m + 3, 2 * i)

                    with dve.Fori(0, KT // 2 - 1) as i:
                        for j in range(2):
                            step(j, j, i)
                    for j in range(2):
                        step(KT - 2 + j, j)
                elif kind == "gdnin":
                    qkv = [t[:, 2 * n:2 * n + 2, :] for t in (q, k, v) for n in range(HEADS // 2)]
                    reciprocal_of_rms(fed_by[name], rstd[:])
                    nc.vector.memset(conv_in[:, :, 0:CONV - 1], 0.0)

                    def gate_chain():
                        a, t = a_row[0:HEADS, :], c_rows[0:HEADS, :]
                        b = a_row[ROW_B:ROW_B + HEADS, :]
                        grow, brow = gate_rows[0:HEADS, :], gate_rows[ROW_B:ROW_B + HEADS, :]
                        dve.wait_ge(evac, g + 1)
                        nc.vector.tensor_scalar(a, a, small[0:HEADS, 1:2], None, op0=ALU.add).then_inc(row_d, 1)
                        cut_lo(u + 2)
                        dve.wait_ge(row_a, 5)
                        nc.vector.scalar_tensor_tensor(a, a, 0.0, t, op0=ALU.max, op1=ALU.add).then_inc(row_d, 1)
                        dve.wait_ge(row_d, 2)
                        nc.vector.tensor_scalar(a, a, small[0:HEADS, 3:4], -1.0, op0=ALU.mult,
                                                op1=ALU.mult).then_inc(row_d, 1)
                        dve.wait_ge(mixer_consts, MIXER_CONSTS)
                        dve.wait_ge(row_d, 3)
                        nc.vector.tensor_tensor_scan(grow, restart[0:HEADS, :], a, 0.0, op0=ALU.mult,
                                                     op1=ALU.add).then_inc(row_d, 1)
                        nc.vector.tensor_scalar(b, b, 1.0, None, op0=ALU.add).then_inc(row_d, 1)
                        dve.wait_ge(row_d, 5)
                        nc.vector.reciprocal(brow, b).then_inc(row_d, 1)
                        chunks = grow.rearrange("h (c t) -> h c t", t=CHUNK)
                        nc.vector.tensor_tensor(a.rearrange("h (c t) -> h c t", t=CHUNK),
                                                chunks[:, :, CHUNK - 1:].broadcast_to([HEADS, SEQ // CHUNK, CHUNK]),
                                                chunks, ALU.subtract).then_inc(row_d, 1)
                        dve.wait_ge(row_a, 7)
                        dve.wait_ge(row_d, 7)
                        nc.vector.tensor_tensor(gate_rows[2 * ROW_B:2 * ROW_B + HEADS, :], brow,
                                                c_rows[ROW_B:ROW_B + HEADS, :], ALU.mult).then_inc(row_d, 1)

                    def times_beta(hd):
                        dve.wait_ge(decay_ready, hd + 1)
                        nc.vector.tensor_tensor(decay_beta[:, hd, :], ps[:, 5, :], decay[:, hd, :],
                                                ALU.mult).then_inc(decay_beta_ready, 1)

                    for n in range(14):
                        dve.wait_ge(unit_done, u + n + 1)
                        b0 = bank_of(g + n)
                        if 8 <= n <= 13:
                            times_beta(n - 8)
                        if n == 0:
                            nc.vector.tensor_tensor(a_row[0:HEADS, :], ps[0:HEADS, b0, :],
                                                    rstd[0:HEADS, :], ALU.mult)
                            rows = slice(ROW_B, ROW_B + HEADS)
                            nc.vector.tensor_tensor(a_row[rows, :], ps[rows, b0, :], rstd[rows, :],
                                                    ALU.mult).then_inc(evac, 1)
                            gate_chain()
                        elif n <= 9:
                            scaled(conv_in[:, :, CONV - 1:], g + n, 2, rstd[:])
                            cut_lo(u + n + 2)
                            dve.wait_ge(tap_ready, n)
                            for j in range(CONV - 1):
                                for o in range(2):
                                    w = j * 3 * HEADS + 2 * (n - 1) + o
                                    steps = 6 * (n - 1) + 2 * j + o
                                    if j:
                                        dve.wait_ge(tap_step, steps - 1)
                                    nc.vector.scalar_tensor_tensor(
                                        qkv[n - 1][:, o, :], conv_in[:, o, j:j + SEQ], conv_w[:, w:w + 1],
                                        qkv[n - 1][:, o, :], op0=ALU.mult, op1=ALU.add).then_inc(tap_step, 1)
                            dve.wait_ge(tap_step, 6 * n)
                            nc.vector.engine_nop().then_inc(conv_ready, 1)
                            if 2 <= n <= 7:
                                dve.wait_ge(l2_rms, n - 1)
                                nc.vector.reciprocal(sq[0][:], sq[0][:])
                                nc.vector.reciprocal(sq[1][:], sq[1][:]).then_inc(l2_inv, 1)
                        else:
                            dst = z[:, 2 * (n - 10):2 * (n - 10) + 2, :] if n <= 12 else q_mem[:]
                            scaled(dst, g + n, 2, rstd[:])
                            cut_lo(u + n + 2)
                        if n == 3:
                            dve.wait_ge(gate_turned, 1)
                            nc.vector.tensor_copy(
                                gate_cols[:, :, :, 0:HEADS],
                                ps[:, 5, :].rearrange("p (t a n) -> p t a n", t=TT, a=4)[:, :, :, 0:HEADS]
                            ).then_inc(cols_ready, 1)
                        if 7 <= n <= 12:
                            hd = n - 7
                            dve.wait_ge(cols_ready, 1)
                            dve.wait_ge(g_spread, hd + 1)
                            dst = decay[:, hd, :].rearrange("p (t n) -> p t n", t=TT)
                            nc.vector.tensor_tensor(dst, ps[:, 4, :].rearrange("p (t n) -> p t n", t=TT),
                                                    gate_cols[:, :, 0, hd:hd + 1].broadcast_to([P, TT, P]),
                                                    ALU.subtract).then_inc(diff_step, 1)
                            dve.wait_ge(diff_step, hd + 1)
                            nc.vector.tensor_scalar(decay[:, hd, :], decay[:, hd, :], 0.0, None,
                                                    op0=ALU.min).then_inc(diff_ready, 1)
                elif kind == "gdn":
                    memory_attention(0, q_mem)
                    A, B, C, D = (heads_of(b) for b in SETS)
                    nc.vector.memset(state[0][:], 0.0).then_inc(state_zero, 1)
                    for p in range(TT):
                        cs = pair_cols(p)

                        def col(a):
                            return over_columns(gate_cols[:, p, a, 0:HEADS], P)

                        dve.wait_ge(gram, p + 1)
                        nc.vector.tensor_tensor(decay_beta[:, :, cs], A, decay_beta[:, :, cs],
                                                ALU.mult).then_inc(low_ready, 1)
                        dve.wait_ge(k_turned, p + 1)
                        nc.vector.tensor_tensor(k_tail[:], C, col(3), ALU.mult)
                        if p:
                            output_scale(p - 1)
                        nc.vector.tensor_tensor(k_rhs[:], C, col(2), ALU.mult).then_inc(k_tok_ready, 1)
                        dve.wait_ge(qk, p + 1)
                        nc.vector.tensor_tensor(decay[:, :, cs], B, decay[:, :, cs],
                                                ALU.mult).then_inc(qk_ready, 1)
                        dve.wait_ge(v_turned, p + 1)
                        if p:
                            dve.wait_ge(o_scaled, p)
                        nc.vector.tensor_tensor(v_rhs[:], D, col(1), ALU.mult).then_inc(v_tok_ready, 1)
                        for lv in range(1, HEADS):
                            n = 5 * p + lv
                            dve.wait_ge(z_prod, n)
                            nc.vector.tensor_tensor(inv_t[:], inv_t[:], B, ALU.subtract).then_inc(inv_t_ready, 1)
                        dve.wait_ge(w_prod, p + 1)
                        nc.vector.tensor_copy(k[:, :, cs], B).then_inc(w_ready, 1)
                        for c in range(2):
                            n = 2 * p + c
                            rows = slice(CHUNK * c, CHUNK * (c + 1))
                            dve.wait_ge(ws_prod, n + 1)
                            nc.vector.tensor_tensor(v_new[rows], v[rows, :, cs], A[rows],
                                                    ALU.subtract).then_inc(v_new_ready, 1)
                            dve.wait_ge(state_prod, n + 1)
                            dve.wait_ge(state_decayed, n + 1)
                            st = state[(n + 1) % 2]
                            nc.vector.tensor_tensor(st[:], st[:], C, ALU.add).then_inc(state_ready, 1)
                    output_scale(TT - 1)
                elif kind == "wout":
                    qs, qm = (q, q_mem) if idx == 0 else (fq, fq_mem)
                    for c in range(KT):
                        src = qs[:, c, :] if c < HEADS else qm[:, c - HEADS, :]
                        dve.wait_ge(mix_hi, KT * idx + c + 1)
                        nc.vector.tensor_tensor(x_lo[:, c, :], src, x_hi[:, c, :].bitcast(F32),
                                                ALU.subtract).then_inc(mix_ready, 1)
                    for n in range(KT // 2):
                        dve.wait_ge(unit_done, u + n + 1)
                        b0 = bank_of(g + n)
                        hs = h[:, 2 * n:2 * n + 2, :]
                        nc.vector.tensor_tensor(hs, ps[:, b0:b0 + 2, :], hs, ALU.add).then_inc(evac, 1)
                        if n == KT // 2 - 1:
                            for c in (KT - 2, KT - 1):
                                feed_lo(name, x_lo[:, c, :], h[:, c, :], gains[:, gain + c:gain + c + 1],
                                        x_hi[:, c, :], c)
                        cut_lo(u + n + 2)
                        if n == KT // 2 - 2:
                            for c in range(KT - 2):
                                feed_lo(name, x_lo[:, c, :], h[:, c, :], gains[:, gain + c:gain + c + 1],
                                        x_hi[:, c, :], c)
                elif kind == "kv":
                    reciprocal_of_rms(fed_by[name], rstd[:])
                    for n in range(1 + HEADS):
                        dve.wait_ge(unit_done, u + n + 1)
                        if n == HEADS:
                            c = KT - 1
                            feed_lo(name, x_lo[:, c, :], h[:, c, :], gains[:, gain + c:gain + c + 1],
                                    x_hi[:, c, :], c)
                        if n == 0:
                            fx, ft, one = (t[0:HEADS, :] for t in (f_x, f_t, f_one))
                            nc.vector.memset(one, 1.0)
                            nc.vector.tensor_tensor(fx, ps[0:HEADS, bank_of(g), :], rstd[0:HEADS, :],
                                                    ALU.mult).then_inc(evac, 1)
                            dve.wait_ge(evac, g + 1)
                            nc.vector.tensor_scalar(fx, fx, small[0:HEADS, 2:3], None, op0=ALU.add).then_inc(f_d, 1)
                            cut_lo(u + 2)
                            dve.wait_ge(f_a, 3)
                            nc.vector.scalar_tensor_tensor(fx, fx, 0.0, ft, op0=ALU.min,
                                                           op1=ALU.subtract).then_inc(f_d, 1)
                            dve.wait_ge(f_d, 2)
                            nc.vector.tensor_tensor_scan(c_rows[0:HEADS, :], one, fx, 0.0, op0=ALU.mult,
                                                         op1=ALU.add).then_inc(f_d, 1)
                        else:
                            if n >= 3:
                                dve.wait_ge(kv_spilled[(n - 1) % 2], 16 * ((n - 1) // 2))
                            scaled(kv_out[(n - 1) % 2][:], g + n, 2, rstd[:])
                            cut_lo(u + n + 2)
                        if n == HEADS - 1:
                            for c in range(KT - 1):
                                feed_lo(name, x_lo[:, c, :], h[:, c, :], gains[:, gain + c:gain + c + 1],
                                        x_hi[:, c, :], c)
                elif kind == "foxin":
                    reciprocal_of_rms(fed_by[name], rstd[:])
                    for n in range(4):
                        dve.wait_ge(unit_done, u + n + 1)
                        scaled(fq[:, 2 * n:2 * n + 2, :] if n < 3 else fq_mem[:], g + n, 2, rstd[:])
                        cut_lo(u + n + 2)
                elif kind == "fox":
                    dve.wait_ge(c_turned, 1)
                    nc.vector.tensor_copy(c_cols[:, :, 0:HEADS],
                                          ps[:, 4, 0:TT * 8].rearrange("p (t n) -> p t n", t=TT)[:, :, 0:HEADS]
                                          ).then_inc(c_cols_ready, 1)
                    for hd in range(HEADS):
                        dve.wait_ge(fv_turned, hd + 1)
                        nc.vector.tensor_copy(fv[:, :, hd * P:(hd + 1) * P],
                                              ps[:, 6 + hd % 2, :].rearrange("p (t n) -> p t n", t=TT)
                                              ).then_inc(fv_ready, 1)
                    memory_attention(1, fq_mem)
                    for n in range(HEADS * TT + 3):
                        if n < HEADS * TT:
                            i = n % TT
                            w = (i + 1) * P
                            dve.wait_ge(f_score, n + 1)
                            dve.wait_ge(fb_masked, n + 1)
                            if n >= 4:
                                dve.wait_ge(f_turned, n - 3)
                            nc.vector.scalar_tensor_tensor(fp[n % 4][:, 0:w], ps[:, 4 + n % 2, 0:w], HEAD ** -0.5,
                                                           bias_ts[n % 3][:, 0:w], op0=ALU.mult,
                                                           op1=ALU.add).then_inc(f_biased, 1)
                            dve.wait_ge(f_biased, n + 1)
                            nc.vector.tensor_reduce(f_stat[:, n % 4, 0:1], fp[n % 4][:, 0:w], AX_X, ALU.max,
                                                    negate=True).then_inc(f_max, 1)
                        if 1 <= n <= HEADS * TT:
                            m = n - 1
                            w = (m % TT + 1) * P
                            dve.wait_ge(f_exp, m + 1)
                            nc.vector.reciprocal(f_stat[:, m % 4, 2:3], f_stat[:, m % 4, 1:2]).then_inc(f_inv, 1)
                            dve.wait_ge(f_inv, m + 1)
                            nc.vector.tensor_scalar(fp[m % 4][:, 0:w], fp[m % 4][:, 0:w],
                                                    f_stat[:, m % 4, 2:3], None, op0=ALU.mult).then_inc(f_norm, 1)
                        if n >= 3 and (n - 3) % TT == TT - 1:
                            m = n - 3
                            dve.wait_ge(f_pv, m + 1)
                            hd = m // TT
                            nc.vector.tensor_copy(fq[:, hd, :], ps[:, 2 + hd % 2, :]).then_inc(f_out, 1)
                elif kind == "final":
                    for c in range(KT):
                        dve.wait_ge(y_turned, c + 1)
                        nc.vector.tensor_copy(y_tok[:, :, c * P:(c + 1) * P],
                                              ps[:, 6 + c % 2, :].rearrange("p (t n) -> p t n", t=TT)).then_inc(y_moved, 1)
                    dve.wait_ge(rms_ready, sums_before[last_update] + 1)
                    nc.vector.reciprocal(small[:, 4:8], small[:, 4:8]).then_inc(y_scale, 1)
                    dve.wait_ge(y_scale, 1)
                    dve.wait_ge(y_moved, KT)
                    for t in (0, 2):
                        nc.vector.tensor_scalar(y_tok[:, t, :], y_tok[:, t, :], small[:, 4 + t:5 + t],
                                                None, op0=ALU.mult).then_inc(y_ready, 1)

        @block.gpsimd
        def _(pool):
            made = [0]

            def constant(ins):
                made[0] += 1
                ins.then_inc(consts, 1)
                pool.wait_ge(consts, made[0])

            constant(nc.gpsimd.memset(ident[:], 0.0))
            constant(nc.gpsimd.affine_select(out=ident[:], in_=ident[:], compare_op=ALU.not_equal, fill=1.0,
                                             base=0, pattern=[[-1, P]], channel_multiplier=1))

            def add_square(name, b, c, tokens=SEQ, i=0):
                done = KT * sums_before[name] + c
                pool.wait_ge(sq_ready, done + 1 + 2 * i)
                if done >= 1:
                    pool.wait_ge(sum_ready, done + 2 * i)
                nc.gpsimd.tensor_tensor(square_sum[:, 0:tokens], square_sum[:, 0:tokens],
                                        gate_up[:, b, 0, 0:tokens], ALU.add).then_inc(sum_ready, 1)

            def clear_sum(name):
                n = sums_before[name]
                if n:
                    pool.wait_ge(sum_done, n)
                nc.gpsimd.memset(square_sum[:], 0.0).then_inc(sum_zero, 1)
                pool.wait_ge(sum_zero, n + 1)

            for name in phases:
                kind, idx = name[:-1], int(name[-1])
                if kind in ("memtr", "xtr"):
                    clear_sum(name)
                    for c in range(KT):
                        add_square(name, c % 2, c, MEM_LEN if kind == "memtr" else SEQ)
                elif kind == "up":
                    def step(n, j, i=0):
                        pool.wait_ge(silu_ready, NP * idx + n + 1 + 2 * i)
                        nc.gpsimd.tensor_tensor(gate_up[:, j, 0, :], gate_up[:, j, 0, :],
                                                gate_up[:, j, 1, :], ALU.mult).then_inc(prod_ready, 1)

                    with pool.Fori(0, NP // 2) as i:
                        for j in range(2):
                            step(j, j, i)
                elif kind == "down":
                    clear_sum(name)
                    with pool.Fori(0, KT // 2) as i:
                        for j in range(2):
                            add_square(name, j, j, i=i)
                elif kind == "gdnin":
                    pool.wait_ge(sum_done, sums_before[fed_by[name]])
                    pool.wait_ge(evac, first_group[name])
                    n_made = [0]

                    def constant2(ins):
                        n_made[0] += 1
                        ins.then_inc(mixer_consts, 1)
                        pool.wait_ge(mixer_consts, n_made[0])

                    def keep(dst, compare, base, pattern, multiplier, fill):
                        constant2(nc.gpsimd.affine_select(out=dst, in_=dst, compare_op=compare, fill=fill, base=base,
                                                          pattern=pattern, channel_multiplier=multiplier))

                    constant2(nc.gpsimd.memset(gate_rows[:], 0.0))
                    constant2(nc.gpsimd.memset(restart[:], 1.0))
                    constant2(nc.gpsimd.memset(restart[:].rearrange("p (c t) -> p c t", t=CHUNK)[:, :, 0:1], 0.0))
                    constant2(nc.gpsimd.memset(pick[:], 0.0))
                    for r0 in (0, ROW_B):
                        keep(pick[r0:r0 + ROW_B], ALU.not_equal, 0, [[-1, HEADS], [0, P]], 1, 1.0)
                    constant2(nc.gpsimd.memset(causal[:], 1.0))
                    keep(causal[:], ALU.is_ge, 0, [[1, P]], -1, 0.0)
                    constant2(nc.gpsimd.memset(causal[0:CHUNK, CHUNK:P], 0.0))
                    constant2(nc.gpsimd.memset(level[:], 1.0))
                    for l in range(HEADS):
                        s = 1 << l
                        dst = level[:, l, :].rearrange("p (a b) -> p a b", b=2 * s)
                        keep(dst, ALU.is_ge, 0, [[-2 * s, P // (2 * s)], [0, 2 * s]], 1, 0.0)
                        keep(dst, ALU.is_ge, s - 1, [[2 * s, P // (2 * s)], [0, 2 * s]], -1, 0.0)
                        constant2(nc.gpsimd.memset(dst[:, :, 0:s], 0.0))
                    assert n_made[0] == MIXER_CONSTS, n_made
                    qkv = [t[:, 2 * n:2 * n + 2, :] for t in (q, k) for n in range(HEADS // 2)]
                    for n in range(1, HEADS + 1):
                        pool.wait_ge(act_ready, n)
                        for o in range(2):
                            tile = qkv[n - 1][:, o, :]
                            last = nc.gpsimd.tensor_tensor(sq[o][:], tile, tile, ALU.mult)
                        last.then_inc(l2_sq, 1)
                        pool.wait_ge(l2_inv, n)
                        for o in range(2):
                            tile = qkv[n - 1][:, o, :]
                            last = nc.gpsimd.tensor_tensor(tile, tile, sq[o][:], ALU.mult)
                        last.then_inc(l2_done, 1)
                        pool.wait_ge(l2_done, n)
                    for hd in range(HEADS):
                        pool.wait_ge(decay_exp, hd + 1)
                        dst = decay[:, hd, :].rearrange("p (t n) -> p t n", t=TT)
                        nc.gpsimd.tensor_tensor(dst, dst, over_heads(causal[:], TT), ALU.mult).then_inc(decay_ready, 1)
                elif kind == "gdn":
                    def gate_output(p):
                        cs = pair_cols(p)
                        pool.wait_ge(o_scaled, p + 1)
                        nc.gpsimd.tensor_tensor(q[:, :, cs], o_pair[:], z[:, :, cs], ALU.mult).then_inc(o_done, 1)

                    for p in range(TT):
                        cs = pair_cols(p)
                        pool.wait_ge(low_ready, p + 1)
                        if p:
                            pool.wait_ge(w_prod, p)
                        nc.gpsimd.tensor_tensor(below[0][:], decay_beta[:, :, cs], over_heads(level[:, 0, :]),
                                                ALU.mult).then_inc(below_step, 1)
                        pool.wait_ge(below_step, p + 1)
                        nc.gpsimd.tensor_tensor(inv_t[:], over_heads(ident[:]), below[0][:],
                                                ALU.subtract).then_inc(inv0_ready, 1)
                        for lv in range(1, HEADS):
                            n = 5 * p + lv
                            if lv == 2:
                                pool.wait_ge(inv0_ready, p + 1)
                            if n > 2:
                                pool.wait_ge(y_prod, n - 2)
                            nc.gpsimd.tensor_tensor(below[lv % 2][:], decay_beta[:, :, cs],
                                                    over_heads(level[:, lv, :]), ALU.mult).then_inc(below_ready, 1)
                            if lv == 2:
                                pool.wait_ge(exp_g_ready, p + 1)
                                pool.wait_ge(qk, p + 1)
                                nc.gpsimd.tensor_tensor(q[:, :, cs], q[:, :, cs], exp_g[:],
                                                        ALU.mult).then_inc(q_head_ready, 1)
                            if lv == 3 and p:
                                gate_output(p - 1)
                        for c in range(2):
                            n = 2 * p + c
                            if n:
                                pool.wait_ge(state_ready, n)
                                pool.wait_ge(o_prod, n)
                            else:
                                pool.wait_ge(state_zero, 1)
                            last_g = exp_g[:, :, CHUNK * (c + 1) - 1:CHUNK * (c + 1)].broadcast_to([P, HEADS, P])
                            nc.gpsimd.tensor_tensor(state[(n + 1) % 2][:], state[n % 2][:], last_g,
                                                    ALU.mult).then_inc(state_decayed, 1)
                    gate_output(TT - 1)
                elif kind == "wout":
                    clear_sum(name)
                    for c in range(KT):
                        add_square(name, c % 2, c)
                elif kind == "kv":
                    for n in range(HEADS):
                        pool.wait_ge(evac, first_group[name] + n + 2)
                        pool.dma_start(kv_spill[:, 2 * n:2 * n + 2, :], kv_out[n % 2][:]).then_inc(kv_spilled[n % 2], 16)
                elif kind == "fox":
                    pool.wait_ge(evac, first_group["foxin0"] + 4)
                    nc.gpsimd.memset(fpick[:], 0.0).then_inc(fox_consts, 1)
                    pool.wait_ge(fox_consts, 1)
                    nc.gpsimd.affine_select(out=fpick[:], in_=fpick[:], compare_op=ALU.not_equal, fill=1.0,
                                            base=0, pattern=[[-1, HEADS], [0, P]],
                                            channel_multiplier=1).then_inc(fox_consts, 1)
                    for n in range(HEADS * TT):
                        i = n % TT
                        dst = bias_ts[n % 3][:, i * P:(i + 1) * P]
                        pool.wait_ge(fb_ready, n + 1)
                        nc.gpsimd.affine_select(out=dst, in_=dst, compare_op=ALU.is_ge, fill=NEG_INF, base=0,
                                                pattern=[[-1, P]], channel_multiplier=1).then_inc(fb_masked, 1)


_INS = ["mem", "x", "ffn1_norm", "ffn1_w_gate_up", "ffn1_w_down", "mix_norm", "ffn2_norm",
        "ffn2_w_gate_up", "ffn2_w_down", "gdn_w_in", "gdn_conv", "gdn_A_log", "gdn_dt_bias",
        "gdn_out_norm", "fox_w_in", "w_out", "mem_norm", "mem_w_kv", "kv_norm", "kv_w", "kv_b_f",
        "final_norm"]

PHASES = ["memtr0", "memkv0", "memkv1", "memvtr0", "xtr0", "up0", "down0", "gdnin0", "gdn0", "wout0",
          "up1", "down1", "kv0", "up2", "down2", "foxin0", "fox0", "wout1", "up3", "down3", "final0"]


def kernel(**inputs):
    import numpy as np
    import concourse.bacc as bacc
    from concourse.bass_utils import run_bass_kernel_spmd

    nc = bacc.Bacc("TRN2", target_bir_lowering=False, num_devices=1)
    arrays, args = {}, []
    for name in _INS:
        a = np.ascontiguousarray(inputs[name])
        arrays[f"in_{name}"] = a
        args.append(nc.dram_tensor(f"in_{name}", a.shape, mybir.dt.from_np(a.dtype), kind="ExternalInput").ap())
    kv_spill = nc.dram_tensor("kv_spill", (P, 2 * HEADS, SEQ), F32, kind="Internal").ap()
    out = nc.dram_tensor("out_0", (1, SEQ, D_MODEL), F32, kind="ExternalOutput").ap()
    build_trunk(nc, *args, kv_spill, out, PHASES)
    r = run_bass_kernel_spmd(nc, [arrays], core_ids=[0])
    return r.results[0]["out_0"]
```

```python
import math
from contextlib import ExitStack

import concourse.bass as bass
from concourse import mybir

F32 = mybir.dt.float32
F32R = mybir.dt.float32r
ALU = mybir.AluOpType
ACT = mybir.ActivationFunctionType
AX_X = mybir.AxisListType.X

P = 128
D_MODEL = 1024
SEQ = 512
DEPTH = 2
HEAD = 128
HEADS = 6
WIDTH = HEADS * HEAD
CONV = 4
CHUNK = 64
MEM_LEN = 256
MEM_HEADS = 4
MEM_HEAD = 64
MEM_WIDTH = MEM_HEADS * MEM_HEAD
FFN = 2816
EPS = 1e-6
NEG_INF = -1e30

KT = D_MODEL // P
TT = SEQ // P
MT = MEM_LEN // P
NP = FFN // P
HALF = NP // 2
FULL_UNIT = KT * 2 * P
DOWN_UNIT = HALF * P
ROW_B = 32

G_FFN1, G_MIX, G_FFN2, G_KV, G_FINAL, G_MEM = 0, 2 * KT, 4 * KT, 6 * KT, 7 * KT, 8 * KT
G_OUT = 9 * KT
GAINS = 9 * KT + 1


def unit_plan(phases):
    first_unit, first_group, sizes = {}, {}, []
    group = 0
    for name in phases:
        kind = name.rstrip("0123456789")
        first_unit[name], first_group[name] = len(sizes), group
        if kind == "memtr":
            group += KT
        elif kind == "memkv":
            sizes += [FULL_UNIT] * 2
            group += 2
        elif kind == "memvtr":
            group += DEPTH
        elif kind == "xtr":
            group += KT
        elif kind == "up":
            sizes += [FULL_UNIT] * NP
            group += NP
        elif kind == "down":
            sizes += [DOWN_UNIT] * (2 * KT)
            group += KT
        elif kind == "gdnin":
            sizes += [KT * P] + [FULL_UNIT] * 13
            group += 14
        elif kind == "foxin":
            sizes += [FULL_UNIT] * 4
            group += 4
        elif kind == "wout":
            sizes += [FULL_UNIT] * (KT // 2)
            group += KT // 2
        elif kind == "kv":
            sizes += [KT * P] + [FULL_UNIT] * HEADS
            group += 1 + HEADS
    return first_unit, first_group, sizes


def build_trunk(nc, mem, x, ffn1_norm, ffn1_gu, ffn1_down, mix_norm, ffn2_norm, ffn2_gu, ffn2_down,
                gdn_w_in, gdn_conv, gdn_a_log, gdn_dt_bias, gdn_out_norm, fox_w_in, w_out,
                mem_norm, mem_w_kv, kv_norm, kv_w, kv_b_f, final_norm, kv_spill, out, phases):
    first_unit, first_group, unit_words = unit_plan(phases)
    units = len(unit_words)

    gain_after = {"memtr0": G_MEM, "xtr0": G_FFN1, "down0": G_MIX, "wout0": G_FFN2, "down1": G_KV,
                  "kv0": G_FFN1 + KT, "down2": G_MIX + KT, "wout1": G_FFN2 + KT, "down3": G_FINAL}
    sums_before, feeds_before = {}, {}
    for name in phases:
        if name in gain_after:
            feeds_before[name] = len(feeds_before)
            if name != "kv0":
                sums_before[name] = len(sums_before)
    last_update = phases[-2]
    gain_after[last_update] = G_FINAL
    fed_by = {"up0": "xtr0", "gdnin0": "down0", "up1": "wout0", "kv0": "down1", "up2": "kv0",
              "foxin0": "down2", "up3": "wout1"}

    with ExitStack() as ctx:
        def sem(name):
            return ctx.enter_context(nc.semaphore(name))

        base = (nc.sbuf_base + 63) // 64 * 64
        space = nc.sbuf_usable_end - base - 64
        ctx.enter_context(nc.sbuf_tensor("arena", [P, space // 4], F32))
        cursor = [base]

        def words(shape):
            n = 1
            for s in shape[1:]:
                n *= s
            return (4 * n + 31) // 32 * 32

        def place(name, shape, dtype=F32, at=None):
            where = cursor[0] if at is None else at
            t = nc.alloc_sbuf_tensor_at(name, shape, dtype, offset=where)
            if at is None:
                cursor[0] += words(shape)
            assert where + words(shape) <= nc.sbuf_usable_end
            return t

        class Region:

            def __init__(self, start, size):
                self.next, self.end = start, start + size

            def put(self, name, shape, dtype=F32):
                t = place(name, shape, dtype, at=self.next)
                self.next += words(shape)
                assert self.next <= self.end, name
                return t

        h = place("h", [P, KT, SEQ])
        ident = place("ident", [P, P])
        ones = place("ones", [P, P])
        gains = place("gains", [P, GAINS])
        conv_w = place("conv_w", [P, CONV * 3 * HEADS])
        eps = place("eps", [P, 2])
        small = place("small", [P, 8])
        rstd = place("rstd", [P, SEQ])
        square_sum = place("square_sum", [P, SEQ])
        c_rows = place("c_rows", [P, SEQ])
        mem_k = place("mem_k", [P, DEPTH, MT, MEM_LEN])
        mem_v = place("mem_v", [P, DEPTH, MT, MEM_WIDTH])
        pair_at = cursor[0]
        PAIR_BYTES = 8224
        gate_up = place("gate_up", [P, 2, 2, SEQ])
        cursor[0] = pair_at + PAIR_BYTES
        raw, w_hi, w_lo, slot_at = [], [], [], []
        for s in range(2):
            slot_at.append(cursor[0])
            raw.append(place(f"raw{s}", [P, FULL_UNIT]))
            w_hi.append(place(f"w_hi{s}", [P, FULL_UNIT], F32R))
            w_lo.append(place(f"w_lo{s}", [P, FULL_UNIT], F32R))
        x_at, X_BYTES = cursor[0], 2 * KT * SEQ * 4
        x_hi = place("x_hi", [P, KT, SEQ], F32R)
        x_lo = place("x_lo", [P, KT, SEQ], F32R)
        h_at, H_BYTES = cursor[0], 2 * NP * SEQ * 4
        hid_hi = place("hid_hi", [P, NP, SEQ], F32R)
        hid_lo = place("hid_lo", [P, NP, SEQ], F32R)

        start = Region(h_at, H_BYTES)
        mem_tok = start.put("mem_tok", [P, MT, D_MODEL])
        x_tok = start.put("x_tok", [P, TT, D_MODEL])
        mem_t = start.put("mem_t", [P, KT, MEM_LEN])
        xm_hi = start.put("xm_hi", [P, KT, MEM_LEN], F32R)
        xm_lo = start.put("xm_lo", [P, KT, MEM_LEN], F32R)
        mem_vt = start.put("mem_vt", [P, DEPTH, MT, MEM_LEN])
        rstd_mem = start.put("rstd_mem", [P, MEM_LEN])
        gain_rows = start.put("gain_rows", [P, P])
        conv_rows = start.put("conv_rows", [P, P])

        mixer = Region(h_at, H_BYTES)
        q = mixer.put("q", [P, HEADS, SEQ])
        k = mixer.put("k", [P, HEADS, SEQ])
        v = mixer.put("v", [P, HEADS, SEQ])
        z = mixer.put("z", [P, HEADS, SEQ])
        q_mem = mixer.put("q_mem", [P, MT, SEQ])
        decay_beta = mixer.put("decay_beta", [P, HEADS, SEQ])
        decay = mixer.put("decay", [P, HEADS, SEQ])
        pick = mixer.put("pick", [P, HEADS, P])
        causal = mixer.put("causal", [P, P])
        level = mixer.put("level", [P, HEADS, P])
        tail = mixer.next
        gate_rows = place("gate_rows", [P, SEQ], at=tail)
        gate_cols = place("gate_cols", [P, TT, 4, 8], at=tail + 2048)
        a_row = place("a_row", [P, SEQ], at=tail + 2560)
        state0 = place("state0", [P, HEADS, P], at=tail + 2560)
        assert tail + 2560 + 3072 <= h_at + H_BYTES
        conv_in = place("conv_in", [P, 2, CONV - 1 + SEQ], at=pair_at)
        sq = place("sq", [P, 2, SEQ], at=pair_at + 4128)
        restart = place("restart", [P, SEQ], at=pair_at + 4128 + 2048)

        core = Region(slot_at[1], x_at - slot_at[1] + X_BYTES)
        inv, inv_t, below, step_y, k_tail, k_rhs, exp_g, v_rhs = (
            [core.put(f"{n}{e}", [P, HEADS, P]) for e in range(2)]
            for n in ("inv", "inv_t", "below", "step_y", "k_tail", "k_rhs", "exp_g", "v_rhs"))
        pair_region = Region(pair_at, PAIR_BYTES)
        v_new = pair_region.put("v_new", [P, HEADS, P])
        o_pair = [pair_region.put("o_pair0", [P, HEADS, P]), core.put("o_pair1", [P, HEADS, P])]
        state = [state0, core.put("state1", [P, HEADS, P])]
        o_sq, o_rms = k_rhs, v_rhs

        att = Region(x_at, X_BYTES)
        mp = [att.put(f"mp{b}", [P, TT, MEM_LEN]) for b in range(2)]
        mpt = att.put("mpt", [P, MT, SEQ])
        m_stat = att.put("m_stat", [P, 2, 4, TT])

        FOX_DEEP = 6
        fox = Region(h_at, H_BYTES)
        fq = fox.put("fq", [P, HEADS, SEQ])
        fk = fox.put("fk", [P, HEADS, SEQ])
        fvt = fox.put("fvt", [P, HEADS, SEQ])
        fq_mem = fox.put("fq_mem", [P, MT, SEQ])
        fv = fox.put("fv", [P, TT, WIDTH])
        fpick = fox.put("fpick", [P, HEADS, P])
        bias_ts = [fox.put(f"bias_ts{b}", [P, SEQ]) for b in range(3)]
        fp = [fox.put(f"fp{b}", [P, SEQ]) for b in range(FOX_DEEP)]
        fpt = [fox.put(f"fpt{b}", [P, SEQ]) for b in range(2)]
        c_cols = fox.put("c_cols", [P, TT, 8])
        f_stat = fox.put("f_stat", [P, FOX_DEEP, 4])
        f_x = place("f_x", [P, SEQ], at=h_at)
        f_t = place("f_t", [P, SEQ], at=h_at + 2048)
        f_one = place("f_one", [P, SEQ], at=h_at + 4096)
        kv_out = [place(f"kv_out{b}", [P, 2, SEQ], at=pair_at + 4096 * b) for b in range(2)]

        end = Region(x_at, X_BYTES)
        y_t = end.put("y_t", [P, KT, SEQ])
        y_tok = end.put("y_tok", [P, TT, D_MODEL])

        ps = ctx.enter_context(nc.psum_tensor("ps", [P, 8, SEQ], F32))

        CONSTS = 2
        MIXER_CONSTS, FOX_CONSTS = 28, 2

        releases = {"wout0": 0, "kv0": 1, "wout1": 2}
        N_REL = KT - 1
        SETS = ((4, 6), (0, 2))

        def heads_of(b):
            return ps[:, b:b + 2, :].rearrange("p b n -> p (b n)")[:, 0:WIDTH].rearrange(
                "p (h n) -> p h n", h=HEADS)

        MIX_ORDER = (*range(HEADS, KT), *range(HEADS))
        values_at = ((), (), (0, 1), (2, 3, 4, 5))

        def step_of(p, lv):
            return (p // 2) * 2 * (HEADS - 1) + 2 * (lv - 1) + p % 2

        def pair_cols(p):
            return slice(p * P, (p + 1) * P)

        def over_columns(a, n):
            return a.rearrange("p (h o) -> p h o", o=1).broadcast_to([P, a.shape[1], n])

        def over_heads(a, n=HEADS):
            return a.rearrange("p (o n) -> p o n", o=1).broadcast_to([P, n, a.shape[1]])

        mem_in, gains_in, x_in, conv_in_sem, small_in = (sem(n) for n in (
            "mem_in", "gains_in", "x_in", "conv_w_in", "small_in"))
        consts = sem("consts")
        dve_consts = sem("dve_consts")
        table_tr, tables = sem("table_tr"), sem("tables")
        raw_in = [sem(f"raw_in{s}") for s in range(2)]
        hi_ready, lo_ready = sem("hi_ready"), sem("lo_ready")
        unit_done = sem("unit_done")
        turned = sem("turned")
        evac = sem("evac")
        sq_ready, sum_zero, sum_ready = sem("sq_ready"), sem("sum_zero"), sem("sum_ready")
        sum_done = sem("sum_done")
        rms_ready, rstd_ready = sem("rms_ready"), sem("rstd_ready")
        x_hi_ready, x_ready = sem("x_hi_ready"), sem("x_ready")
        x_free = sem("x_free")
        silu_ready, prod_ready = sem("silu_ready"), sem("prod_ready")
        hid_hi_ready, hid_ready = sem("hid_hi_ready"), sem("hid_ready")

        mix_hi, mix_ready = sem("mix_hi"), sem("mix_ready")
        tap_ready, tap_step, conv_ready, act_ready = (sem(n) for n in (
            "tap_ready", "tap_step", "conv_ready", "act_ready"))
        l2_sq, l2_sum, l2_log, l2_inv, l2_done = (sem(n) for n in (
            "l2_sq", "l2_sum", "l2_log", "l2_inv", "l2_done"))
        row_a, row_d, gate_turned, cols_ready = (sem(n) for n in (
            "row_a", "row_d", "gate_turned", "cols_ready"))
        g_spread, diff_step, diff_ready, decay_exp, decay_ready, decay_beta_ready = (sem(n) for n in (
            "g_spread", "diff_step", "diff_ready", "decay_exp", "decay_ready", "decay_beta_ready"))
        mixer_consts = sem("mixer_consts")
        ma_score, ma_max, ma_bias, ma_exp, ma_inv, ma_norm, ma_turned, ma_copied, ma_pv, ma_out = (
            sem(n) for n in ("ma_score", "ma_max", "ma_bias", "ma_exp", "ma_inv", "ma_norm",
                             "ma_turned", "ma_copied", "ma_pv", "ma_out"))
        gram, qk, k_turned, v_turned = (sem(n) for n in ("gram", "qk", "k_turned", "v_turned"))
        low_ready, qk_ready, k_tok_ready, v_tok_ready = (sem(n) for n in (
            "low_ready", "qk_ready", "k_tok_ready", "v_tok_ready"))
        below_step, below_ready, inv0_ready = sem("below_step"), sem("below_ready"), sem("inv0_ready")
        inv_turned, inv_ready = sem("inv_turned"), sem("inv_ready")
        y_prod, step_y_ready, z_prod, inv_t_ready = (sem(n) for n in (
            "y_prod", "step_y_ready", "z_prod", "inv_t_ready"))
        u_prod, w_prod, u_ready, w_ready = (sem(n) for n in ("u_prod", "w_prod", "u_ready", "w_ready"))
        pair_g, exp_g_ready, q_head_ready = sem("pair_g"), sem("exp_g_ready"), sem("q_head_ready")
        ws_prod, v_new_ready, state_prod, o_prod = (sem(n) for n in (
            "ws_prod", "v_new_ready", "state_prod", "o_prod"))
        state_zero, state_decayed, state_ready = sem("state_zero"), sem("state_decayed"), sem("state_ready")
        o_copied, o_sq_ready, o_sum, o_log, o_inv, o_scaled, o_done = (sem(n) for n in (
            "o_copied", "o_sq_ready", "o_sum", "o_log", "o_inv", "o_scaled", "o_done"))
        f_a, f_d = sem("f_a"), sem("f_d")
        fox_consts, c_turned, c_cols_ready, fv_turned, fv_ready = (sem(n) for n in (
            "fox_consts", "c_turned", "c_cols_ready", "fv_turned", "fv_ready"))
        fc_spread, fb_ready, fb_masked, f_score, f_biased, f_max, f_exp, f_inv, f_norm = (
            sem(n) for n in ("fc_spread", "fb_ready", "fb_masked", "f_score", "f_biased", "f_max",
                             "f_exp", "f_inv", "f_norm"))
        f_turned, f_copied, f_pv, f_out = (sem(n) for n in ("f_turned", "f_copied", "f_pv", "f_out"))
        y_gained, y_turned, y_moved = sem("y_gained"), sem("y_turned"), sem("y_moved")
        y_scale = sem("y_scale")
        y_ready, y_ready_odd, out_done = sem("y_ready"), sem("y_ready_odd"), sem("out_done")
        kv_spilled, kv_back = [sem(f"kv_spilled{b}") for b in range(2)], sem("kv_back")

        mem_rows = mem.rearrange("b (t p) d -> p (b t) d", p=P)
        x_rows = x.rearrange("b (t p) d -> p (b t) d", p=P)
        out_rows = out.rearrange("b (t p) d -> p (b t) d", p=P)

        def blocks(w):
            return w.rearrange("(k p) n -> p k n", p=P)

        ffn_gu = [blocks(w[l]) for l in range(DEPTH) for w in (ffn1_gu, ffn2_gu)]
        ffn_down = [blocks(w[l]) for l in range(DEPTH) for w in (ffn1_down, ffn2_down)]

        def slot(u0):
            return u0 % 2

        def weights_landed(u0, i=0):
            return 32 * (u0 // 2 + 1) + 32 * i

        block = ctx.enter_context(nc.Block())

        @block.sync
        def _(sp):
            def load(u0, parts, i=0):
                if u0 >= 2:
                    sp.wait_ge(lo_ready, u0 - 1 + 2 * i)
                for dst, src in parts:
                    sp.dma_start(dst, src).then_inc(raw_in[slot(u0)], 16)

            def load_cols(u0, w, col, i=0, width=2 * P):
                dst = raw[slot(u0)][:, 0:KT * width].rearrange("p (k n) -> p k n", k=KT)
                half = KT // 2
                load(u0, [(dst[:, a:a + half, :], w[:, a:a + half, bass.ds(col, width)])
                          for a in (0, half)], i)

            def load_gate_up(u0, w, n, i=0):
                dst = raw[slot(u0)][:].rearrange("p (k g n) -> p k g n", k=KT, g=2)
                load(u0, [(dst[:, :, g, :], w[:, :, bass.ds(g * FFN + n, P)]) for g in (0, 1)], i)

            def load_down(u0, w, half, n, i=0):
                dst = raw[slot(u0)][:, 0:DOWN_UNIT].rearrange("p (k n) -> p k n", k=HALF)
                cut = HALF // 2
                load(u0, [(dst[:, a:b, :], w[:, half * HALF + a:half * HALF + b, bass.ds(n, P)])
                          for a, b in ((0, cut), (cut, HALF))], i)

            for name in phases:
                kind, idx = name[:-1], int(name[-1])
                u = first_unit[name]
                if kind == "memtr":
                    sp.dma_start(mem_tok[:], mem_rows).then_inc(mem_in, 16)
                elif kind == "memkv":
                    if idx == 0:
                        sp.wait_ge(x_in, 16 * TT)
                    for n in range(2):
                        load_cols(u + n, blocks(mem_w_kv[idx]), n * MEM_WIDTH)
                elif kind == "up":
                    for n in range(2):
                        load_gate_up(u + n, ffn_gu[idx], n * P)
                    with sp.Fori(0, NP // 2 - 1) as i:
                        for j in range(2):
                            load_gate_up(u + 2 + j, ffn_gu[idx], (2 * i + (2 + j)) * P, i)
                elif kind == "down":
                    with sp.Fori(0, KT) as m:
                        for half in range(2):
                            load_down(u + half, ffn_down[idx], half, m * P, m)
                elif kind == "gdnin":
                    w = blocks(gdn_w_in[0])
                    dst = raw[slot(u)][:, 0:KT * P].rearrange("p (k n) -> p k n", k=KT)
                    a_col = 4 * WIDTH
                    load(u, [(dst[:, :, 0:ROW_B], w[:, :, a_col:a_col + ROW_B]),
                             (dst[:, :, ROW_B:P], w[:, :, a_col + HEADS:a_col + HEADS + P - ROW_B])])
                    for n in range(12):
                        load_cols(u + 1 + n, w, n * 2 * P)
                    load_cols(u + 13, w, 4 * WIDTH + 2 * HEADS)
                elif kind == "foxin":
                    for n in range(4):
                        load_cols(u + n, blocks(fox_w_in[0]), n * 2 * P)
                elif kind == "wout":
                    for n in range(KT // 2):
                        if idx == 0 and n == 1:
                            sp.wait_ge(w_prod, TT)
                        load_cols(u + n, blocks(w_out[idx]), n * 2 * P)
                elif kind == "kv":
                    w = blocks(kv_w)
                    dst = raw[slot(u)][:, 0:KT * P].rearrange("p (k n) -> p k n", k=KT)
                    load(u, [(dst[:, :, 0:HEADS], w[:, :, 2 * WIDTH:2 * WIDTH + HEADS]),
                             (dst[:, :, HEADS:P], w[:, :, 0:P - HEADS])])
                    for n in range(HEADS):
                        load_cols(u + 1 + n, w, n * 2 * P)
                elif kind == "final":
                    for t in range(TT):
                        sp.wait_ge((y_ready, y_ready_odd)[t % 2], t // 2 + 1)
                        sp.dma_start(out_rows[:, t, :], y_tok[:, t, :]).then_inc(out_done, 16)
                    sp.wait_ge(out_done, 16 * TT)

        @block.tensor
        def _(pe):
            def bank_of(g0):
                return 2 * (g0 % 2)

            def bank_free(g0, i=0):
                if g0 >= 2:
                    pe.wait_ge(evac, g0 - 1 + 2 * i)

            def split_products(dst, hi, lo, xh, xl, first, last):
                nc.tensor.matmul(dst, hi, xh, start=first, stop=False)
                nc.tensor.matmul(dst, hi, xl, start=False, stop=False)
                return nc.tensor.matmul(dst, lo, xh, start=False, stop=last)

            def unit(u0, g0, xh, xl, i=0, outs=2, tokens=SEQ, feed=None, ready=x_ready, release=False,
                     order=range(KT)):
                s, width = slot(u0), outs * P
                pe.wait_ge(lo_ready, u0 + 1 + 2 * i)
                bank_free(g0, i)
                for i_c, c in enumerate(order):
                    if feed is not None:
                        pe.wait_ge(ready, feed + i_c + 1)
                    for o in range(outs):
                        at = c * width + o * P
                        last = split_products(ps[:, bank_of(g0) + o, 0:tokens], w_hi[s][:, at:at + P],
                                              w_lo[s][:, at:at + P], xh[:, c, :], xl[:, c, :],
                                              i_c == 0, i_c == KT - 1)
                    if release and i_c < KT - 1:
                        last.then_inc(x_free, 1)
                last.then_inc(unit_done, 1)

            def down_tile(u0, g0, hid_wait=None, i=0):
                for half in range(2):
                    s = slot(u0 + half)
                    pe.wait_ge(lo_ready, u0 + half + 1 + 4 * i)
                    if half == 0:
                        bank_free(g0, i)
                    if hid_wait is not None:
                        pe.wait_ge(hid_ready, hid_wait + (half + 1) * HALF)
                    for c in range(HALF):
                        n = half * HALF + c
                        last = split_products(ps[:, bank_of(g0), :], w_hi[s][:, c * P:(c + 1) * P],
                                              w_lo[s][:, c * P:(c + 1) * P], hid_hi[:, n, :],
                                              hid_lo[:, n, :], n == 0, n == NP - 1)
                    last.then_inc(unit_done, 1)

            def spread_sum(name, tokens=SEQ):
                pe.wait_ge(sum_ready, KT * (sums_before[name] + 1))
                nc.tensor.matmul(ps[:, 4, 0:tokens], ones[:], square_sum[:, 0:tokens],
                                 start=True, stop=True).then_inc(sum_done, 1)

            def memory_attention(idx, qm):
                def scores(hd):
                    t, r0, n = hd // 2, MEM_HEAD * (hd % 2), MEM_HEADS * idx + hd
                    if hd >= 2:
                        pe.wait_ge(ma_exp, n - 1)
                    for i in range(TT):
                        last = nc.tensor.matmul(
                            ps[:, (4, 2)[hd % 2] + i // 2, (i % 2) * MEM_LEN:(i % 2 + 1) * MEM_LEN],
                            qm[r0:r0 + MEM_HEAD, t, i * P:(i + 1) * P],
                            mem_k[r0:r0 + MEM_HEAD, idx, t, :], start=True, stop=True)
                    last.then_inc(ma_score, 1)

                scores(0)
                scores(1)
                for hd in range(MEM_HEADS):
                    n, r0 = MEM_HEADS * idx + hd, MEM_HEAD * (hd % 2)
                    pe.wait_ge(ma_norm, n + 1)
                    if n == 0:
                        pe.wait_ge(decay_beta_ready, HEADS)
                    if hd:
                        pe.wait_ge(ma_copied, n)
                    for st in range(MT):
                        for i in range(TT):
                            last = nc.tensor.transpose(ps[:, 6 + st, i * P:(i + 1) * P],
                                                       mp[hd % 2][:, i, st * P:(st + 1) * P], ident[:])
                    last.then_inc(ma_turned, 1)
                    if hd + 2 < MEM_HEADS:
                        scores(hd + 2)
                    pe.wait_ge(ma_copied, n + 1)
                    if hd >= 2:
                        pe.wait_ge(ma_out, n - 1)
                    for st in range(MT):
                        last = nc.tensor.matmul(ps[r0:r0 + MEM_HEAD, hd % 2, :],
                                                mem_v[:, idx, st, hd * MEM_HEAD:(hd + 1) * MEM_HEAD],
                                                mpt[:, st, :], start=st == 0, stop=st == MT - 1)
                    last.then_inc(ma_pv, 1)

            for name in phases:
                kind, idx = name[:-1], int(name[-1])
                u, g = first_unit[name], first_group[name]
                if kind == "memtr":
                    pe.wait_ge(consts, CONSTS)
                    pe.wait_ge(mem_in, 16)
                    for c in range(KT):
                        bank_free(g + c)
                        for t in range(MT):
                            last = nc.tensor.transpose(ps[:, bank_of(g + c), t * P:(t + 1) * P],
                                                       mem_tok[:, t, c * P:(c + 1) * P], ident[:])
                        last.then_inc(turned, 1)
                        if c == 0:
                            pe.wait_ge(gains_in, 16 * 7)
                            nc.tensor.transpose(ps[:, 4, 0:GAINS], gain_rows[0:GAINS, :], ident[0:GAINS, 0:GAINS]).then_inc(table_tr, 1)
                            pe.wait_ge(conv_in_sem, 16)
                            nc.tensor.transpose(ps[:, 5, 0:4 * 18], conv_rows[0:72, :], ident[0:72, 0:72]).then_inc(table_tr, 1)
                    spread_sum("memtr0", MEM_LEN)
                elif kind == "memkv":
                    for n in range(2):
                        unit(u + n, g + n, xm_hi, xm_lo, tokens=MEM_LEN,
                             feed=0 if (idx, n) == (0, 0) else None)
                elif kind == "memvtr":
                    for l in range(DEPTH):
                        pe.wait_ge(evac, g)
                        bank_free(g + l)
                        for t in range(MT):
                            for c in range(MT):
                                last = nc.tensor.transpose(
                                    ps[:, bank_of(g + l), (t * MT + c) * P:(t * MT + c + 1) * P],
                                    mem_vt[:, l, c, t * P:(t + 1) * P], ident[:])
                        last.then_inc(turned, 1)
                elif kind == "xtr":
                    for t in range(TT):
                        pe.wait_ge(x_in, 16 * TT)
                    for c in range(KT):
                        bank_free(g + c)
                        for t in range(TT):
                            last = nc.tensor.transpose(ps[:, bank_of(g + c), t * P:(t + 1) * P],
                                                       x_tok[:, t, c * P:(c + 1) * P], ident[:])
                        last.then_inc(turned, 1)
                elif kind == "up":
                    unit(u, g, x_hi, x_lo, feed=KT * feeds_before[fed_by[name]])
                    if fed_by[name] != "kv0":
                        spread_sum(fed_by[name])
                    unit(u + 1, g + 1, x_hi, x_lo)
                    with pe.Fori(0, NP // 2 - 1) as i:
                        for j in range(2):
                            unit(u + 2 + j, g + 2 + j, x_hi, x_lo, i)
                elif kind == "down":
                    down_tile(u, g, hid_wait=NP * idx)
                    down_tile(u + 2, g + 1)
                    with pe.Fori(0, KT // 2 - 1) as i:
                        for j in range(2):
                            down_tile(u + 4 + 2 * j, g + 2 + j, i=i)
                elif kind == "gdnin":
                    for n in range(14):
                        unit(u + n, g + n, x_hi, x_lo, outs=1 if n == 0 else 2,
                             feed=KT * feeds_before[fed_by[name]] if n == 0 else None)
                        if n == 0:
                            spread_sum(fed_by[name])
                        if 3 <= n <= 8:
                            pe.wait_ge(l2_sq, n - 2)
                            for o in range(2):
                                last = nc.tensor.matmul(ps[:, 6 + o, :], ones[:], sq[:, o, :],
                                                        start=True, stop=True)
                            last.then_inc(l2_sum, 1)
                        if n == 3:
                            pe.wait_ge(row_d, 8)
                            for t in range(TT):
                                last = nc.tensor.transpose(ps[:, 5, t * P:(t + 1) * P],
                                                           gate_rows[:, t * P:(t + 1) * P], ident[:])
                            last.then_inc(gate_turned, 1)
                        if 8 <= n <= 13:
                            hd = n - 8
                            b0 = 4 + 2 * (hd % 2)
                            pe.wait_ge(mixer_consts, MIXER_CONSTS)
                            if hd == 0:
                                pe.wait_ge(cols_ready, 1)
                            elif hd == 1:
                                pe.wait_ge(l2_log, HEADS)
                            else:
                                pe.wait_ge(decay_beta_ready, hd - 1)
                            nc.tensor.matmul(ps[:, b0, :], pick[0:HEADS, hd, :], gate_rows[0:HEADS, :],
                                             start=True, stop=True)
                            nc.tensor.matmul(ps[:, b0 + 1, :], pick[ROW_B:ROW_B + HEADS, hd, :],
                                             gate_rows[ROW_B:ROW_B + HEADS, :],
                                             start=True, stop=True).then_inc(g_spread, 1)
                elif kind == "gdn":
                    first, second = ([heads_of(s[i]) for s in SETS] for i in range(2))
                    pe.wait_ge(evac, first_group["gdnin0"] + 14)
                    pe.wait_ge(decay_beta_ready, HEADS - 1)
                    memory_attention(0, q_mem)
                    pe.wait_ge(ma_out, MEM_HEADS)
                    pe.wait_ge(l2_done, HEADS)
                    pe.wait_ge(act_ready, 9)

                    def each_head(dst, lhs, rhs, signal):
                        for hd in range(HEADS):
                            last = nc.tensor.matmul(dst[:, hd, :], lhs(hd), rhs(hd), start=True, stop=True)
                        last.then_inc(signal, 1)

                    def turn_heads(dst, src, signal):
                        for hd in range(HEADS):
                            last = nc.tensor.transpose(dst[:, hd, :], src(hd), ident[:])
                        last.then_inc(signal, 1)

                    def output_sum(p):
                        b0, flat = SETS[p % 2][1], o_sq[p % 2][:].rearrange("p h n -> p (h n)")
                        pe.wait_ge(o_sq_ready, p + 1)
                        nc.tensor.matmul(ps[:, b0, :], ones[:], flat[:, 0:SEQ], start=True, stop=True)
                        nc.tensor.matmul(ps[:, b0 + 1, 0:WIDTH - SEQ], ones[:], flat[:, SEQ:WIDTH],
                                         start=True, stop=True).then_inc(o_sum, 1)

                    def gram_product(p):
                        cs = pair_cols(p)
                        if p >= 2:
                            pe.wait_ge(v_new_ready if p % 2 == 0 else state_ready, 4 * (p // 2))
                        each_head(first[p % 2], lambda hd: k[:, hd, cs], lambda hd: k[:, hd, cs], gram)

                    def turn_keys(p):
                        cs = pair_cols(p)
                        if p >= 2:
                            pe.wait_ge(o_log, p - 1)
                        turn_heads(second[p % 2], lambda hd: k[:, hd, cs], k_turned)

                    def turn_values(p):
                        cs = pair_cols(p)
                        pe.wait_ge(low_ready, p + 1)
                        turn_heads(first[p % 2], lambda hd: v[:, hd, cs], v_turned)

                    def query_product(p):
                        cs = pair_cols(p)
                        pe.wait_ge(k_tok_ready, p + 1)
                        each_head(second[p % 2], lambda hd: k[:, hd, cs], lambda hd: q[:, hd, cs], qk)

                    def spread_g(p):
                        cs = pair_cols(p)
                        pe.wait_ge(v_tok_ready, p + 1)
                        each_head(first[p % 2], lambda hd: pick[0:HEADS, hd, :],
                                  lambda hd: gate_rows[0:HEADS, cs], pair_g)

                    for p0 in range(0, TT, 2):
                        both = (p0, p0 + 1)
                        gram_product(p0)
                        turn_keys(p0)
                        gram_product(p0 + 1)
                        if p0:
                            output_sum(p0 - 1)
                        turn_values(p0)
                        query_product(p0)
                        turn_keys(p0 + 1)
                        turn_values(p0 + 1)
                        query_product(p0 + 1)
                        spread_g(p0)
                        spread_g(p0 + 1)
                        for lv in range(1, HEADS):
                            for p in both:
                                e, n = p % 2, step_of(p, lv)
                                if lv == 1:
                                    pe.wait_ge(inv0_ready, p + 1)
                                    pe.wait_ge(exp_g_ready, p + 1)
                                else:
                                    pe.wait_ge(inv_t_ready, n - 1)
                                turn_heads(first[e], lambda hd: inv_t[e][:, hd, :], inv_turned)
                            for p in both:
                                e, n = p % 2, step_of(p, lv)
                                pe.wait_ge(inv_ready, n + 1)
                                pe.wait_ge(below_ready, n + 1)
                                each_head(first[e], lambda hd: below[e][:, hd, :], lambda hd: inv[e][:, hd, :],
                                          y_prod)
                            for p in both:
                                e, n = p % 2, step_of(p, lv)
                                if lv == 1:
                                    pe.wait_ge(qk_ready, p + 1)
                                pe.wait_ge(step_y_ready, n + 1)
                                each_head(second[e], lambda hd: step_y[e][:, hd, :],
                                          lambda hd: inv_t[e][:, hd, :], z_prod)
                        for p in both:
                            e = p % 2
                            pe.wait_ge(inv_t_ready, step_of(p, HEADS - 1) + 1)
                            each_head(first[e], lambda hd: inv_t[e][:, hd, :], lambda hd: v_rhs[e][:, hd, :], u_prod)
                            each_head(second[e], lambda hd: k_rhs[e][:, hd, :], lambda hd: inv_t[e][:, hd, :], w_prod)
                        pe.wait_ge(u_ready, p0 + 2)
                        pe.wait_ge(w_ready, p0 + 2)
                        pe.wait_ge(q_head_ready, p0 + 2)
                        for n in range(2 * p0, 2 * p0 + 4):
                            p, c = divmod(n, 2)
                            e, r0 = p % 2, CHUNK * c
                            rows, tok = slice(r0, r0 + CHUNK), slice(p * P + r0, p * P + r0 + CHUNK)
                            st = state[n % 2]
                            if n:
                                pe.wait_ge(state_ready, n)
                            else:
                                pe.wait_ge(state_zero, 1)
                            for hd in range(HEADS):
                                last = nc.tensor.matmul(first[0][rows, hd, :], k[:, hd, tok], st[:, hd, :],
                                                        start=True, stop=True)
                            last.then_inc(ws_prod, 1)
                            for hd in range(HEADS):
                                nc.tensor.matmul(second[e][:, hd, rows], st[:, hd, :], q[:, hd, tok],
                                                 start=hd % TT == 0, stop=False)
                            pe.wait_ge(v_new_ready, n + 1)
                            for hd in range(HEADS):
                                last = nc.tensor.matmul(first[1][:, hd, :], k_tail[e][rows, hd, :],
                                                        v_new[rows, hd, :], start=True, stop=True)
                            last.then_inc(state_prod, 1)
                            for hd in range(HEADS):
                                last = nc.tensor.matmul(second[e][:, hd, rows], v_new[rows, hd, :],
                                                        decay[rows, hd, tok], start=False,
                                                        stop=hd in (TT - 1, HEADS - 1))
                            last.then_inc(o_prod, 1)
                            if (e, c) == (1, 0):
                                output_sum(p0)
                    output_sum(TT - 1)
                elif kind == "wout":
                    for n in range(KT // 2):
                        unit(u + n, g + n, x_hi, x_lo, feed=KT * idx if n == 0 else None,
                             ready=mix_ready, release=n == KT // 2 - 1,
                             order=MIX_ORDER if n == 0 else range(KT))
                elif kind == "kv":
                    for n in range(1 + HEADS):
                        unit(u + n, g + n, x_hi, x_lo, outs=1 if n == 0 else 2,
                             feed=KT * feeds_before[fed_by[name]] if n == 0 else None,
                             release=n == HEADS)
                        if n == 0:
                            spread_sum(fed_by[name])
                elif kind == "foxin":
                    for n in range(4):
                        unit(u + n, g + n, x_hi, x_lo,
                             feed=KT * feeds_before[fed_by[name]] if n == 0 else None)
                        if n == 0:
                            spread_sum(fed_by[name])
                        if n == 1:
                            pe.wait_ge(rms_ready, sums_before["down2"] + 1)
                            for t in range(TT):
                                last = nc.tensor.transpose(ps[:, 4, t * 8:t * 8 + HEADS],
                                                           c_rows[0:HEADS, t * P:(t + 1) * P],
                                                           ident[0:HEADS, 0:HEADS])
                            last.then_inc(c_turned, 1)
                        if n == 2:
                            pe.wait_ge(kv_back, 32)
                        for hd in values_at[n]:
                            if hd >= 2:
                                pe.wait_ge(fv_ready, hd - 1)
                            for t in range(TT):
                                last = nc.tensor.transpose(ps[:, 6 + hd % 2, t * P:(t + 1) * P],
                                                           fvt[:, hd, t * P:(t + 1) * P], ident[:])
                            last.then_inc(fv_turned, 1)
                elif kind == "fox":
                    pe.wait_ge(fv_ready, HEADS)
                    pe.wait_ge(c_cols_ready, 1)
                    pe.wait_ge(evac, first_group["foxin0"] + 4)
                    memory_attention(1, fq_mem)
                    pe.wait_ge(ma_out, 2 * MEM_HEADS)
                    pe.wait_ge(fox_consts, FOX_CONSTS)

                    def spread_c(hd):
                        if hd >= 2:
                            pe.wait_ge(fb_ready, TT * (hd - 1))
                        nc.tensor.matmul(ps[:, hd % 2, :], fpick[0:HEADS, hd, :], c_rows[0:HEADS, :],
                                         start=True, stop=True).then_inc(fc_spread, 1)

                    spread_c(0)
                    for n in range(HEADS * TT + 4):
                        if n < HEADS * TT:
                            hd, i = divmod(n, TT)
                            if n % TT == 2 and hd + 1 < HEADS:
                                spread_c(hd + 1)
                            if n >= 2:
                                pe.wait_ge(f_biased, n - 1)
                            nc.tensor.matmul(ps[:, 4 + n % 2, 0:(i + 1) * P], fq[:, hd, i * P:(i + 1) * P],
                                             fk[:, hd, 0:(i + 1) * P], start=True, stop=True).then_inc(f_score, 1)
                        if 3 <= n < HEADS * TT + 3:
                            m = n - 3
                            hd, i = divmod(m, TT)
                            pe.wait_ge(f_norm, m + 1)
                            if m >= 2:
                                pe.wait_ge(f_copied, m - 1)
                            for s in range(i + 1):
                                last = nc.tensor.transpose(ps[:, 6 + m % 2, s * P:(s + 1) * P],
                                                           fp[m % FOX_DEEP][:, s * P:(s + 1) * P], ident[:])
                            last.then_inc(f_turned, 1)
                        if n >= 4:
                            m = n - 4
                            hd, i = divmod(m, TT)
                            pe.wait_ge(f_copied, m + 1)
                            if i == 0 and hd >= 2:
                                pe.wait_ge(f_out, hd - 1)
                            for s in range(i + 1):
                                last = nc.tensor.matmul(ps[:, 2 + hd % 2, i * P:(i + 1) * P],
                                                        fv[:, s, hd * P:(hd + 1) * P],
                                                        fpt[m % 2][:, s * P:(s + 1) * P],
                                                        start=s == 0, stop=s == i)
                            last.then_inc(f_pv, 1)
                elif kind == "final":
                    for c in range(KT):
                        pe.wait_ge(y_gained, c + 1)
                        if c >= 2:
                            pe.wait_ge(y_moved, c - 1)
                        for t in range(TT):
                            last = nc.tensor.transpose(ps[:, 6 + c % 2, t * P:(t + 1) * P],
                                                       y_t[:, c, t * P:(t + 1) * P], ident[:])
                        last.then_inc(y_turned, 1)
                    pe.wait_ge(sum_ready, KT * (sums_before[last_update] + 1))
                    for t in range(TT):
                        last = nc.tensor.matmul(ps[:, 4, t:t + 1], square_sum[:, t * P:(t + 1) * P],
                                                ones[:, 0:1], start=True, stop=True)
                    last.then_inc(sum_done, 1)

        @block.scalar
        def _(act):
            def round_hi(u, i=0):
                if not isinstance(u, int) or u < units:
                    n, s = unit_words[u], slot(u)
                    act.wait_ge(raw_in[s], weights_landed(u, i))
                    if u >= 2:
                        act.wait_ge(unit_done, u - 1 + 2 * i)
                    nc.scalar.activation(w_hi[s][:, 0:n], raw[s][:, 0:n], ACT.Copy).then_inc(hi_ready, 1)

            def feed_hi(dst, src, gain):
                nc.scalar.activation(dst, src, ACT.Copy, scale=gain).then_inc(x_hi_ready, 1)

            def square_free(name, c, i=0):
                done = KT * sums_before[name] + c
                if done >= 2:
                    act.wait_ge(sum_ready, done - 1 + 2 * i)

            def square(name, b, c, src, tokens=SEQ, looped=False):
                if not looped:
                    square_free(name, c)
                nc.scalar.activation(gate_up[:, b, 0, 0:tokens], src, ACT.Square).then_inc(sq_ready, 1)

            def root_mean_square(name, dst, tokens=SEQ):
                act.wait_ge(sum_done, sums_before[name] + 1)
                nc.scalar.activation(dst, ps[:, 4, 0:tokens], ACT.Sqrt, scale=1.0 / D_MODEL,
                                     bias=eps[:, 0:1]).then_inc(rms_ready, 1)

            def memory_attention(idx):
                if idx == 0:
                    act.wait_ge(evac, first_group["gdnin0"] + 14)

                def exponentials(hd):
                    b = hd % 2
                    act.wait_ge(ma_bias, MEM_HEADS * idx + hd + 1)
                    for i in range(TT):
                        last = nc.scalar.activation(
                            mp[b][:, i, :], ps[:, (4, 2)[b] + i // 2, (i % 2) * MEM_LEN:(i % 2 + 1) * MEM_LEN],
                            ACT.Exp, scale=MEM_HEAD ** -0.5, bias=m_stat[:, b, 1, i:i + 1],
                            accum_out=m_stat[:, b, 2, i:i + 1])
                    last.then_inc(ma_exp, 1)

                exponentials(0)
                for hd in range(MEM_HEADS):
                    n = MEM_HEADS * idx + hd
                    if hd + 1 < MEM_HEADS:
                        exponentials(hd + 1)
                    act.wait_ge(ma_turned, n + 1)
                    if hd:
                        act.wait_ge(ma_pv, n)
                    nc.scalar.activation(mpt[:], ps[:, 6:8, :], ACT.Copy).then_inc(ma_copied, 1)

            def mix_memory_hi(qm):
                for t in range(MT):
                    nc.scalar.activation(x_hi[:, HEADS + t, :], qm[:, t, :], ACT.Copy).then_inc(mix_hi, 1)

            for name in phases:
                kind, idx = name[:-1], int(name[-1])
                u, g = first_unit[name], first_group[name]
                gain = gain_after.get(name)
                if kind == "memtr":
                    row = 0
                    for vec in (ffn1_norm, mix_norm, ffn2_norm, kv_norm, final_norm, mem_norm, gdn_out_norm):
                        flat = vec if len(vec.shape) == 1 else vec.rearrange("a b -> (a b)")
                        n = flat.shape[0] // P
                        act.dma_start(gain_rows[row:row + n, :], flat.rearrange("(r c) -> r c", c=P)).then_inc(gains_in, 16)
                        row += n
                    act.dma_start(conv_rows[0:4 * 18, :], gdn_conv.rearrange("o j (r c) -> (o j r) c", c=P)).then_inc(conv_in_sem, 16)
                    for t in range(TT):
                        act.dma_start(x_tok[:, t, :], x_rows[:, t, :]).then_inc(x_in, 16)
                    act.dma_start(small[0:HEADS, 0:1], gdn_a_log.rearrange("o h -> h o")).then_inc(small_in, 16)
                    act.dma_start(small[0:HEADS, 1:2], gdn_dt_bias.rearrange("o h -> h o")).then_inc(small_in, 16)
                    act.dma_start(small[0:HEADS, 2:3], kv_b_f.rearrange("(h o) -> h o", o=1)).then_inc(small_in, 16)
                    act.wait_ge(tables, 2)
                    for c in range(KT):
                        act.wait_ge(evac, g + c + 1)
                        feed_hi(xm_hi[:, c, :], mem_t[:, c, :], gains[:, gain + c:gain + c + 1])
                        square(name, c % 2, c, mem_t[:, c, :], MEM_LEN)
                    act.wait_ge(dve_consts, 2)
                    round_hi(0)
                    root_mean_square("memtr0", rstd_mem[:], MEM_LEN)
                    round_hi(1)
                elif kind == "memkv":
                    for n in range(2):
                        round_hi(u + n + 2)
                elif kind == "xtr":
                    for c in range(KT):
                        act.wait_ge(evac, g + c + 1)
                        feed_hi(x_hi[:, c, :], h[:, c, :], gains[:, gain + c:gain + c + 1])
                        square(name, c % 2, c, h[:, c, :])
                    act.wait_ge(small_in, 48)
                elif kind == "up":
                    if fed_by[name] != "kv0":
                        root_mean_square(fed_by[name], rstd[:])

                    def step(n, j, i=0):
                        round_hi(u + n + 2, i)
                        act.wait_ge(evac, g + n + 1 + 2 * i)
                        nc.scalar.activation(gate_up[:, j, 0, :], gate_up[:, j, 0, :],
                                             ACT.Silu).then_inc(silu_ready, 1)
                        act.wait_ge(prod_ready, NP * idx + n + 1 + 2 * i)
                        at = n + 2 * i
                        nc.scalar.activation(hid_hi[:, bass.ds(at, 1), :], gate_up[:, j, 0:1, :],
                                             ACT.Copy).then_inc(hid_hi_ready, 1)

                    with act.Fori(0, NP // 2 - 1) as i:
                        for j in range(2):
                            step(j, j, i)
                    for j in range(2):
                        step(NP - 2 + j, j)
                elif kind == "down":
                    def step(m, j, i=0):
                        for half in range(2):
                            round_hi_4(u + 2 * m + half + 2, i)
                        square_free(name, m, i)
                        act.wait_ge(evac, g + m + 1 + 2 * i)
                        c = m + 2 * i
                        act.wait_ge(tables, 2)
                        if name != last_update:
                            feed_hi(x_hi[:, bass.ds(c, 1), :], h[:, bass.ds(c, 1), :],
                                    gains[:, bass.ds(gain + c, 1)])
                        square(name, j, m, h[:, bass.ds(c, 1), :].rearrange("p a n -> p (a n)"), looped=True)

                    def round_hi_4(w, i):
                        round_hi(w, 2 * i)

                    with act.Fori(0, KT // 2 - 1) as i:
                        for j in range(2):
                            step(j, j, i)
                    for j in range(2):
                        step(KT - 2 + j, j)
                elif kind == "gdnin":
                    qkv = [t[:, 2 * n:2 * n + 2, :] for t in (q, k, v) for n in range(HEADS // 2)]

                    for n in range(14):
                        if n == 0:
                            root_mean_square(fed_by[name], rstd[:])
                            round_hi(u + 2)
                            a, t = a_row[0:HEADS, :], c_rows[0:HEADS, :]
                            b = a_row[ROW_B:ROW_B + HEADS, :]
                            act.wait_ge(row_d, 1)
                            nc.scalar.activation(t, a, ACT.Abs).then_inc(row_a, 1)
                            act.wait_ge(row_a, 1)
                            nc.scalar.activation(t, t, ACT.Exp, scale=-1.0).then_inc(row_a, 1)
                            nc.scalar.activation(b, b, ACT.Exp, scale=-1.0).then_inc(row_a, 1)
                            nc.scalar.activation(small[0:HEADS, 3:4], small[0:HEADS, 0:1],
                                                 ACT.Exp).then_inc(row_a, 1)
                            act.wait_ge(row_a, 2)
                            nc.scalar.activation(t, t, ACT.Ln, bias=ones[0:HEADS, 0:1]).then_inc(row_a, 1)
                        elif n <= 9:
                            act.wait_ge(evac, g + n + 1)
                            for o in range(2):
                                tile = 2 * (n - 1) + o
                                last = nc.scalar.activation(
                                    qkv[n - 1][:, o, :], conv_in[:, o, CONV - 1:], ACT.Copy,
                                    scale=conv_w[:, 3 * 3 * HEADS + tile:3 * 3 * HEADS + tile + 1])
                            last.then_inc(tap_ready, 1)
                            round_hi(u + n + 2)
                            if n == 1:
                                act.wait_ge(row_d, 7)
                                nc.scalar.activation(c_rows[ROW_B:ROW_B + HEADS, :], gate_rows[0:HEADS, :],
                                                     ACT.Exp).then_inc(row_a, 1)
                                nc.scalar.activation(gate_rows[3 * ROW_B:3 * ROW_B + HEADS, :],
                                                     a_row[0:HEADS, :], ACT.Exp).then_inc(row_a, 1)
                            if 3 <= n <= 8:
                                act.wait_ge(l2_sum, n - 2)
                                nc.scalar.activation(sq[:], ps[:, 6:8, :], ACT.Ln,
                                                     bias=eps[:, 0:1]).then_inc(l2_log, 1)
                                act.wait_ge(l2_log, n - 2)
                                if n - 2 <= HEADS // 2:
                                    nc.scalar.activation(sq[:], sq[:], ACT.Exp, scale=-0.5,
                                                         bias=eps[:, 1:2]).then_inc(l2_inv, 1)
                                else:
                                    nc.scalar.activation(sq[:], sq[:], ACT.Exp, scale=-0.5).then_inc(l2_inv, 1)
                            act.wait_ge(conv_ready, n)
                            nc.scalar.activation(qkv[n - 1], qkv[n - 1], ACT.Silu).then_inc(act_ready, 1)
                        else:
                            if n < 13:
                                round_hi(u + n + 2)
                            act.wait_ge(evac, g + n + 1)
                            if n <= 12:
                                zt = z[:, 2 * (n - 10):2 * (n - 10) + 2, :]
                                nc.scalar.activation(zt, zt, ACT.Silu).then_inc(act_ready, 1)
                        if 8 <= n <= 13:
                            hd = n - 8
                            act.wait_ge(diff_ready, hd + 1)
                            nc.scalar.activation(decay[:, hd, :], decay[:, hd, :], ACT.Exp).then_inc(decay_exp, 1)
                elif kind == "gdn":
                    memory_attention(0)
                    first, second = ([heads_of(s[i]) for s in SETS] for i in range(2))
                    for p0 in range(0, TT, 2):
                        both = (p0, p0 + 1)
                        for p in both:
                            act.wait_ge(pair_g, p + 1)
                            if p >= 2:
                                act.wait_ge(state_decayed, 2 * (p - 1))
                            nc.scalar.activation(exp_g[p % 2][:], first[p % 2], ACT.Exp).then_inc(exp_g_ready, 1)
                        for lv in range(1, HEADS):
                            for p in both:
                                e, n = p % 2, step_of(p, lv)
                                act.wait_ge(inv_turned, n + 1)
                                if n >= 2:
                                    act.wait_ge(y_prod, n - 1)
                                nc.scalar.activation(inv[e][:], first[e], ACT.Copy).then_inc(inv_ready, 1)
                            for p in both:
                                e, n = p % 2, step_of(p, lv)
                                act.wait_ge(y_prod, n + 1)
                                if n >= 2:
                                    act.wait_ge(z_prod, n - 1)
                                nc.scalar.activation(step_y[e][:], first[e], ACT.Copy).then_inc(step_y_ready, 1)
                        for p in both:
                            act.wait_ge(u_prod, p + 1)
                            nc.scalar.activation(v[:, :, pair_cols(p)], first[p % 2], ACT.Copy).then_inc(u_ready, 1)
                        for p in both:
                            e = p % 2
                            act.wait_ge(o_prod, 2 * (p + 1))
                            if p >= 2:
                                act.wait_ge(o_done, p - 1)
                            nc.scalar.activation(o_pair[e][:], second[e], ACT.Copy).then_inc(o_copied, 1)
                            act.wait_ge(o_copied, p + 1)
                            nc.scalar.activation(o_sq[e][:], o_pair[e][:], ACT.Square).then_inc(o_sq_ready, 1)
                            if p == TT - 1:
                                act.wait_ge(ma_out, MEM_HEADS)
                                act.wait_ge(state_decayed, 2 * TT)
                                mix_memory_hi(q_mem)
                            act.wait_ge(o_sum, p + 1)
                            nc.scalar.activation(o_rms[e][:], second[e], ACT.Ln, scale=1.0 / HEAD,
                                                 bias=eps[:, 0:1]).then_inc(o_log, 1)
                            act.wait_ge(o_log, p + 1)
                            nc.scalar.activation(o_rms[e][:], o_rms[e][:], ACT.Exp, scale=-0.5).then_inc(o_inv, 1)
                    round_hi(first_unit["wout0"] + 1)
                elif kind == "wout":
                    qs, qm = (q, q_mem) if idx == 0 else (fq, fq_mem)
                    if idx == 0:
                        act.wait_ge(o_done, TT)
                    else:
                        act.wait_ge(f_out, HEADS)
                        mix_memory_hi(qm)
                    for c in range(HEADS):
                        nc.scalar.activation(x_hi[:, c, :], qs[:, c, :], ACT.Copy).then_inc(mix_hi, 1)
                    for n in range(KT // 2):
                        act.wait_ge(evac, g + n + 1)
                        if n == KT // 2 - 1:
                            for c in (KT - 2, KT - 1):
                                if c == KT - 2:
                                    act.wait_ge(x_free, N_REL * (releases[name] + 1))
                                feed_hi(x_hi[:, c, :], h[:, c, :], gains[:, gain + c:gain + c + 1])
                        for c in (2 * n, 2 * n + 1):
                            square(name, c % 2, c, h[:, c, :])
                        round_hi(u + n + 2)
                        if n == KT // 2 - 2:
                            for c in range(KT - 2):
                                act.wait_ge(x_free, N_REL * releases[name] + c + 1)
                                feed_hi(x_hi[:, c, :], h[:, c, :], gains[:, gain + c:gain + c + 1])
                elif kind == "kv":
                    root_mean_square(fed_by[name], rstd[:])
                    for n in range(1 + HEADS):
                        if n == HEADS:
                            act.wait_ge(unit_done, u + n + 1)
                            c = KT - 1
                            feed_hi(x_hi[:, c, :], h[:, c, :], gains[:, gain + c:gain + c + 1])
                        round_hi(u + n + 2)
                        if n == 0:
                            t = f_t[0:HEADS, :]
                            act.wait_ge(f_d, 1)
                            nc.scalar.activation(t, f_x[0:HEADS, :], ACT.Abs).then_inc(f_a, 1)
                            act.wait_ge(f_a, 1)
                            nc.scalar.activation(t, t, ACT.Exp, scale=-1.0).then_inc(f_a, 1)
                            act.wait_ge(f_a, 2)
                            nc.scalar.activation(t, t, ACT.Ln, bias=ones[0:HEADS, 0:1]).then_inc(f_a, 1)
                        if n == HEADS - 1:
                            for c in range(KT - 1):
                                act.wait_ge(x_free, N_REL * releases[name] + c + 1)
                                feed_hi(x_hi[:, c, :], h[:, c, :], gains[:, gain + c:gain + c + 1])
                elif kind == "foxin":
                    root_mean_square(fed_by[name], rstd[:])
                    for b in range(2):
                        act.wait_ge(kv_spilled[b], 16 * (HEADS // 2))
                    act.dma_start(fk[:], kv_spill[:, 0:HEADS, :]).then_inc(kv_back, 16)
                    act.dma_start(fvt[:], kv_spill[:, HEADS:2 * HEADS, :]).then_inc(kv_back, 16)
                    for n in range(4):
                        act.wait_ge(evac, g + n + 1)
                        round_hi(u + n + 2)
                elif kind == "fox":
                    memory_attention(1)

                    def bias_of(n):
                        hd, i = divmod(n, TT)
                        if i == 0:
                            act.wait_ge(fc_spread, hd + 1)
                        if n >= 3:
                            act.wait_ge(f_biased, n - 2)
                        nc.scalar.activation(bias_ts[n % 3][:, 0:(i + 1) * P], ps[:, hd % 2, 0:(i + 1) * P],
                                             ACT.Identity, scale=-1.0,
                                             bias=c_cols[:, i, hd:hd + 1]).then_inc(fb_ready, 1)

                    bias_of(0)
                    bias_of(1)
                    for n in range(HEADS * TT + 3):
                        if n < HEADS * TT:
                            i = n % TT
                            act.wait_ge(f_max, n + 1)
                            nc.scalar.activation(fp[n % FOX_DEEP][:, 0:(i + 1) * P], fp[n % FOX_DEEP][:, 0:(i + 1) * P],
                                                 ACT.Exp, bias=f_stat[:, n % FOX_DEEP, 0:1],
                                                 accum_out=f_stat[:, n % FOX_DEEP, 1:2]).then_inc(f_exp, 1)
                        if n + 2 < HEADS * TT:
                            bias_of(n + 2)
                        if n >= 3:
                            m = n - 3
                            i = m % TT
                            act.wait_ge(f_turned, m + 1)
                            if m >= 2:
                                act.wait_ge(f_pv, m - 1)
                            nc.scalar.activation(fpt[m % 2][:, 0:(i + 1) * P], ps[:, 6 + m % 2, 0:(i + 1) * P],
                                                 ACT.Copy).then_inc(f_copied, 1)
                elif kind == "final":
                    root_mean_square(last_update, small[:, 4:8], TT)
                    for t in (1, 3):
                        act.wait_ge(y_moved, KT)
                        act.wait_ge(y_scale, 1)
                        nc.scalar.activation(y_tok[:, t, :], y_tok[:, t, :], ACT.Copy,
                                             scale=small[:, 4 + t:5 + t]).then_inc(y_ready_odd, 1)

        @block.vector
        def _(dve):
            def cut_lo(u, i=0):
                if u < units:
                    n, s = unit_words[u], slot(u)
                    dve.wait_ge(hi_ready, u + 1 + 2 * i)
                    nc.vector.tensor_tensor(w_lo[s][:, 0:n], raw[s][:, 0:n],
                                            w_hi[s][:, 0:n].bitcast(F32), ALU.subtract).then_inc(lo_ready, 1)

            def feed_lo(name, dst, src, gain, hi, c, i=0):
                dve.wait_ge(x_hi_ready, KT * feeds_before[name] + c + 1 + 2 * i)
                nc.vector.scalar_tensor_tensor(dst, src, gain, hi.bitcast(F32), op0=ALU.mult,
                                               op1=ALU.subtract).then_inc(x_ready, 1)

            def bank_of(g0):
                return 2 * (g0 % 2)

            def output_scale(p):
                dve.wait_ge(o_inv, p + 1)
                e = p % 2
                nc.vector.scalar_tensor_tensor(o_pair[e][:], o_pair[e][:], gains[:, G_OUT:G_OUT + 1], o_rms[e][:],
                                               op0=ALU.mult, op1=ALU.mult).then_inc(o_scaled, 1)

            def reciprocal_of_rms(name, dst):
                n = sums_before[name] + 1
                dve.wait_ge(rms_ready, n)
                nc.vector.reciprocal(dst, dst).then_inc(rstd_ready, 1)
                dve.wait_ge(rstd_ready, n)

            def scaled(dst, g0, outs, scale, tokens=SEQ, signal=None):
                src = ps[:, bank_of(g0):bank_of(g0) + outs, 0:tokens]
                by = scale.rearrange("p (o n) -> p o n", o=1).broadcast_to([P, outs, tokens])
                nc.vector.tensor_tensor(dst, src, by, ALU.mult).then_inc(evac, 1)

            nc.vector.memset(ones[:], 1.0).then_inc(dve_consts, 1)
            nc.vector.memset(eps[:, 0:1], EPS)
            nc.vector.memset(eps[:, 1:2], -0.5 * math.log(HEAD)).then_inc(dve_consts, 1)

            def times_beta(hd):
                dve.wait_ge(decay_ready, hd + 1)
                nc.vector.tensor_tensor(decay_beta[:, hd, :], ps[:, 5 + 2 * (hd % 2), :], decay[:, hd, :],
                                        ALU.mult).then_inc(decay_beta_ready, 1)

            def memory_attention(idx, qm):
                def negative_max(hd):
                    n, b = MEM_HEADS * idx + hd, hd % 2
                    dve.wait_ge(ma_score, n + 1)
                    bank = (4, 2)[b]
                    src = ps[:, bank:bank + 2, :].rearrange("p b (i m) -> p (b i) m", i=2)
                    nc.vector.tensor_reduce(m_stat[:, b, 0, :], src, AX_X, ALU.max,
                                            negate=True).then_inc(ma_max, 1)
                    dve.wait_ge(ma_max, n + 1)
                    nc.vector.tensor_scalar(m_stat[:, b, 1, :], m_stat[:, b, 0, :], MEM_HEAD ** -0.5, None,
                                            op0=ALU.mult).then_inc(ma_bias, 1)

                def results(hd):
                    r0 = MEM_HEAD * (hd % 2)
                    dve.wait_ge(ma_pv, MEM_HEADS * idx + hd + 1)
                    nc.vector.tensor_copy(qm[r0:r0 + MEM_HEAD, hd // 2, :],
                                          ps[r0:r0 + MEM_HEAD, hd % 2, :]).then_inc(ma_out, 1)

                negative_max(0)
                negative_max(1)
                if idx == 0:
                    times_beta(HEADS - 1)
                for hd in range(MEM_HEADS):
                    n, b = MEM_HEADS * idx + hd, hd % 2
                    dve.wait_ge(ma_exp, n + 1)
                    nc.vector.reciprocal(m_stat[:, b, 3, :], m_stat[:, b, 2, :]).then_inc(ma_inv, 1)
                    dve.wait_ge(ma_inv, n + 1)
                    nc.vector.tensor_tensor(mp[b][:], mp[b][:], over_columns(m_stat[:, b, 3, :], MEM_LEN),
                                            ALU.mult).then_inc(ma_norm, 1)
                    if hd + 2 < MEM_HEADS:
                        negative_max(hd + 2)
                    if hd:
                        results(hd - 1)
                results(MEM_HEADS - 1)

            def mix_memory_lo(idx, qm):
                for t in range(MT):
                    dve.wait_ge(mix_hi, KT * idx + t + 1)
                    nc.vector.tensor_tensor(x_lo[:, HEADS + t, :], qm[:, t, :],
                                            x_hi[:, HEADS + t, :].bitcast(F32), ALU.subtract).then_inc(mix_ready, 1)

            for name in phases:
                kind, idx = name[:-1], int(name[-1])
                u, g = first_unit[name], first_group[name]
                gain = gain_after.get(name)
                if kind == "memtr":
                    for c in range(KT):
                        dve.wait_ge(turned, c + 1)
                        nc.vector.tensor_copy(mem_t[:, c, :], ps[:, bank_of(g + c), 0:MEM_LEN]).then_inc(evac, 1)
                        if c == 0:
                            dve.wait_ge(table_tr, 1)
                            nc.vector.tensor_copy(gains[:], ps[:, 4, 0:GAINS]).then_inc(tables, 1)
                            dve.wait_ge(table_tr, 2)
                            nc.vector.tensor_copy(conv_w[:], ps[:, 5, 0:4 * 18]).then_inc(tables, 1)
                            dve.wait_ge(tables, 2)
                        if c >= 1:
                            feed_lo(name, xm_lo[:, c - 1, :], mem_t[:, c - 1, :],
                                    gains[:, gain + c - 1:gain + c], xm_hi[:, c - 1, :], c - 1)
                    c = KT - 1
                    feed_lo(name, xm_lo[:, c, :], mem_t[:, c, :], gains[:, gain + c:gain + c + 1],
                            xm_hi[:, c, :], c)
                    cut_lo(0)
                elif kind == "memkv":
                    for n in range(2):
                        if (idx, n) == (0, 0):
                            reciprocal_of_rms("memtr0", rstd_mem[:])
                        dve.wait_ge(unit_done, u + n + 1)
                        dst = mem_k[:, idx] if n == 0 else mem_vt[:, idx]
                        scaled(dst, g + n, 2, rstd_mem[:], MEM_LEN)
                        cut_lo(u + n + 2)
                elif kind == "memvtr":
                    for l in range(DEPTH):
                        dve.wait_ge(turned, 2 * KT + l + 1)
                        nc.vector.tensor_copy(mem_v[:, l].rearrange("p t n -> p (t n)"),
                                              ps[:, bank_of(g + l), :]).then_inc(evac, 1)
                elif kind == "xtr":
                    for c in range(KT + 1):
                        if c < KT:
                            dve.wait_ge(turned, KT + c + 1)
                            nc.vector.tensor_copy(h[:, c, :], ps[:, bank_of(g + c), :]).then_inc(evac, 1)
                            if c == KT // 2:
                                cut_lo(1)
                        if c >= 1:
                            feed_lo(name, x_lo[:, c - 1, :], h[:, c - 1, :],
                                    gains[:, gain + c - 1:gain + c], x_hi[:, c - 1, :], c - 1)
                elif kind == "up":
                    if fed_by[name] != "kv0":
                        reciprocal_of_rms(fed_by[name], rstd[:])
                    else:
                        for b in range(2):
                            dve.wait_ge(kv_spilled[b], 16 * (HEADS // 2))

                    def step(n, j, i=0):
                        dve.wait_ge(unit_done, u + n + 1 + 2 * i)
                        scaled(gate_up[:, j], g + n, 2, rstd[:])
                        cut_lo(u + n + 2, i)
                        dve.wait_ge(hid_hi_ready, NP * idx + n + 1 + 2 * i)
                        at = n + 2 * i
                        nc.vector.tensor_tensor(hid_lo[:, bass.ds(at, 1), :], gate_up[:, j, 0:1, :],
                                                hid_hi[:, bass.ds(at, 1), :].bitcast(F32),
                                                ALU.subtract).then_inc(hid_ready, 1)

                    with dve.Fori(0, NP // 2 - 1) as i:
                        for j in range(2):
                            step(j, j, i)
                    for j in range(2):
                        step(NP - 2 + j, j)
                elif kind == "down":
                    def step(m, j, i=0):
                        dve.wait_ge(unit_done, u + 2 * m + 1 + 4 * i)
                        cut_lo(u + 2 * m + 2, 2 * i)
                        dve.wait_ge(unit_done, u + 2 * m + 2 + 4 * i)
                        c = m + 2 * i
                        nc.vector.scalar_tensor_tensor(
                            h[:, bass.ds(c, 1), :], ps[:, bank_of(g + m):bank_of(g + m) + 1, :], 0.5,
                            h[:, bass.ds(c, 1), :], op0=ALU.mult, op1=ALU.add).then_inc(evac, 1)
                        if name != last_update:
                            feed_lo(name, x_lo[:, bass.ds(c, 1), :], h[:, bass.ds(c, 1), :],
                                    gains[:, bass.ds(gain + c, 1)], x_hi[:, bass.ds(c, 1), :], m, i)
                        else:
                            dve.wait_ge(evac, g + m + 1 + 2 * i)
                            nc.vector.tensor_scalar(y_t[:, bass.ds(c, 1), :], h[:, bass.ds(c, 1), :],
                                                    gains[:, bass.ds(gain + c, 1)], None,
                                                    op0=ALU.mult).then_inc(y_gained, 1)
                        cut_lo(u + 2 * m + 3, 2 * i)

                    with dve.Fori(0, KT // 2 - 1) as i:
                        for j in range(2):
                            step(j, j, i)
                    for j in range(2):
                        step(KT - 2 + j, j)
                elif kind == "gdnin":
                    qkv = [t[:, 2 * n:2 * n + 2, :] for t in (q, k, v) for n in range(HEADS // 2)]
                    reciprocal_of_rms(fed_by[name], rstd[:])
                    nc.vector.memset(conv_in[:, :, 0:CONV - 1], 0.0)

                    def gate_chain():
                        a, t = a_row[0:HEADS, :], c_rows[0:HEADS, :]
                        b = a_row[ROW_B:ROW_B + HEADS, :]
                        grow, brow = gate_rows[0:HEADS, :], gate_rows[ROW_B:ROW_B + HEADS, :]
                        dve.wait_ge(evac, g + 1)
                        nc.vector.tensor_scalar(a, a, small[0:HEADS, 1:2], None, op0=ALU.add).then_inc(row_d, 1)
                        cut_lo(u + 2)
                        dve.wait_ge(row_a, 5)
                        nc.vector.scalar_tensor_tensor(a, a, 0.0, t, op0=ALU.max, op1=ALU.add).then_inc(row_d, 1)
                        dve.wait_ge(row_d, 2)
                        nc.vector.tensor_scalar(a, a, small[0:HEADS, 3:4], -1.0, op0=ALU.mult,
                                                op1=ALU.mult).then_inc(row_d, 1)
                        dve.wait_ge(mixer_consts, MIXER_CONSTS)
                        dve.wait_ge(row_d, 3)
                        nc.vector.tensor_tensor_scan(grow, restart[0:HEADS, :], a, 0.0, op0=ALU.mult,
                                                     op1=ALU.add).then_inc(row_d, 1)
                        nc.vector.tensor_scalar(b, b, 1.0, None, op0=ALU.add).then_inc(row_d, 1)
                        dve.wait_ge(row_d, 5)
                        nc.vector.reciprocal(brow, b).then_inc(row_d, 1)
                        chunks = grow.rearrange("h (c t) -> h c t", t=CHUNK)
                        nc.vector.tensor_tensor(a.rearrange("h (c t) -> h c t", t=CHUNK),
                                                chunks[:, :, CHUNK - 1:].broadcast_to([HEADS, SEQ // CHUNK, CHUNK]),
                                                chunks, ALU.subtract).then_inc(row_d, 1)

                    def beta_decay_row():
                        dve.wait_ge(row_a, 7)
                        dve.wait_ge(row_d, 7)
                        nc.vector.tensor_tensor(gate_rows[2 * ROW_B:2 * ROW_B + HEADS, :],
                                                gate_rows[ROW_B:ROW_B + HEADS, :],
                                                c_rows[ROW_B:ROW_B + HEADS, :], ALU.mult).then_inc(row_d, 1)

                    for n in range(14):
                        dve.wait_ge(unit_done, u + n + 1)
                        b0 = bank_of(g + n)
                        if n == 0:
                            nc.vector.tensor_tensor(a_row[0:HEADS, :], ps[0:HEADS, b0, :],
                                                    rstd[0:HEADS, :], ALU.mult)
                            rows = slice(ROW_B, ROW_B + HEADS)
                            nc.vector.tensor_tensor(a_row[rows, :], ps[rows, b0, :], rstd[rows, :],
                                                    ALU.mult).then_inc(evac, 1)
                            gate_chain()
                        elif n <= 9:
                            scaled(conv_in[:, :, CONV - 1:], g + n, 2, rstd[:])
                            if n == 1:
                                cut_lo(u + n + 2)
                            dve.wait_ge(tap_ready, n)
                            for j in range(CONV - 1):
                                for o in range(2):
                                    w = j * 3 * HEADS + 2 * (n - 1) + o
                                    steps = 6 * (n - 1) + 2 * j + o
                                    if j:
                                        dve.wait_ge(tap_step, steps - 1)
                                    nc.vector.scalar_tensor_tensor(
                                        qkv[n - 1][:, o, :], conv_in[:, o, j:j + SEQ], conv_w[:, w:w + 1],
                                        qkv[n - 1][:, o, :], op0=ALU.mult, op1=ALU.add).then_inc(tap_step, 1)
                            dve.wait_ge(tap_step, 6 * n)
                            nc.vector.engine_nop().then_inc(conv_ready, 1)
                            if n == 1:
                                beta_decay_row()
                            else:
                                cut_lo(u + n + 2)
                        else:
                            dst = z[:, 2 * (n - 10):2 * (n - 10) + 2, :] if n <= 12 else q_mem[:]
                            scaled(dst, g + n, 2, rstd[:])
                            if n < 13:
                                cut_lo(u + n + 2)
                        if n == 3:
                            dve.wait_ge(gate_turned, 1)
                            nc.vector.tensor_copy(
                                gate_cols[:, :, :, 0:HEADS],
                                ps[:, 5, :].rearrange("p (t a n) -> p t a n", t=TT, a=4)[:, :, :, 0:HEADS]
                            ).then_inc(cols_ready, 1)
                        if 9 <= n <= 13:
                            times_beta(n - 9)
                        if 8 <= n <= 13:
                            hd = n - 8
                            dve.wait_ge(cols_ready, 1)
                            dve.wait_ge(g_spread, hd + 1)
                            dst = decay[:, hd, :].rearrange("p (t n) -> p t n", t=TT)
                            nc.vector.tensor_tensor(dst, ps[:, 4 + 2 * (hd % 2), :].rearrange("p (t n) -> p t n", t=TT),
                                                    gate_cols[:, :, 0, hd:hd + 1].broadcast_to([P, TT, P]),
                                                    ALU.subtract).then_inc(diff_step, 1)
                            dve.wait_ge(diff_step, hd + 1)
                            nc.vector.tensor_scalar(decay[:, hd, :], decay[:, hd, :], 0.0, None,
                                                    op0=ALU.min).then_inc(diff_ready, 1)
                elif kind == "gdn":
                    memory_attention(0, q_mem)
                    first, second = ([heads_of(s[i]) for s in SETS] for i in range(2))
                    nc.vector.memset(state[0][:], 0.0).then_inc(state_zero, 1)

                    def col(p, a):
                        return over_columns(gate_cols[:, p, a, 0:HEADS], P)

                    def lower(p):
                        cs = pair_cols(p)
                        dve.wait_ge(gram, p + 1)
                        nc.vector.tensor_tensor(decay_beta[:, :, cs], first[p % 2], decay_beta[:, :, cs],
                                                ALU.mult).then_inc(low_ready, 1)

                    def token_keys(p):
                        e = p % 2
                        dve.wait_ge(k_turned, p + 1)
                        nc.vector.tensor_tensor(k_tail[e][:], second[e], col(p, 3), ALU.mult)
                        if p >= 2:
                            dve.wait_ge(o_sum, p - 1)
                        nc.vector.tensor_tensor(k_rhs[e][:], second[e], col(p, 2), ALU.mult).then_inc(k_tok_ready, 1)

                    def token_values(p):
                        e = p % 2
                        dve.wait_ge(v_turned, p + 1)
                        if p >= 2:
                            dve.wait_ge(o_scaled, p - 1)
                        nc.vector.tensor_tensor(v_rhs[e][:], first[e], col(p, 1), ALU.mult).then_inc(v_tok_ready, 1)

                    def decayed_scores(p):
                        cs = pair_cols(p)
                        dve.wait_ge(qk, p + 1)
                        nc.vector.tensor_tensor(decay[:, :, cs], second[p % 2], decay[:, :, cs],
                                                ALU.mult).then_inc(qk_ready, 1)

                    for p0 in range(0, TT, 2):
                        both = (p0, p0 + 1)
                        lower(p0)
                        token_keys(p0)
                        lower(p0 + 1)
                        token_values(p0)
                        decayed_scores(p0)
                        if p0:
                            output_scale(p0 - 1)
                        token_keys(p0 + 1)
                        token_values(p0 + 1)
                        decayed_scores(p0 + 1)
                        for lv in range(1, HEADS):
                            for p in both:
                                e, n = p % 2, step_of(p, lv)
                                dve.wait_ge(z_prod, n + 1)
                                nc.vector.tensor_tensor(inv_t[e][:], inv_t[e][:], second[e],
                                                        ALU.subtract).then_inc(inv_t_ready, 1)
                        for p in both:
                            dve.wait_ge(w_prod, p + 1)
                            nc.vector.tensor_copy(k[:, :, pair_cols(p)], second[p % 2]).then_inc(w_ready, 1)
                        for n in range(2 * p0, 2 * p0 + 4):
                            p, c = divmod(n, 2)
                            rows = slice(CHUNK * c, CHUNK * (c + 1))
                            dve.wait_ge(ws_prod, n + 1)
                            nc.vector.tensor_tensor(v_new[rows], v[rows, :, pair_cols(p)], first[0][rows],
                                                    ALU.subtract).then_inc(v_new_ready, 1)
                            dve.wait_ge(state_prod, n + 1)
                            dve.wait_ge(state_decayed, n + 1)
                            st = state[(n + 1) % 2]
                            nc.vector.tensor_tensor(st[:], st[:], first[1], ALU.add).then_inc(state_ready, 1)
                        output_scale(p0)
                    mix_memory_lo(0, q_mem)
                    output_scale(TT - 1)
                elif kind == "wout":
                    qs, qm = (q, q_mem) if idx == 0 else (fq, fq_mem)
                    if idx:
                        mix_memory_lo(idx, qm)
                    for c in range(HEADS):
                        dve.wait_ge(mix_hi, KT * idx + MT + c + 1)
                        nc.vector.tensor_tensor(x_lo[:, c, :], qs[:, c, :], x_hi[:, c, :].bitcast(F32),
                                                ALU.subtract).then_inc(mix_ready, 1)
                    if idx == 0:
                        cut_lo(u + 1)
                    for n in range(KT // 2):
                        dve.wait_ge(unit_done, u + n + 1)
                        b0 = bank_of(g + n)
                        hs = h[:, 2 * n:2 * n + 2, :]
                        nc.vector.tensor_tensor(hs, ps[:, b0:b0 + 2, :], hs, ALU.add).then_inc(evac, 1)
                        if n == KT // 2 - 1:
                            for c in (KT - 2, KT - 1):
                                feed_lo(name, x_lo[:, c, :], h[:, c, :], gains[:, gain + c:gain + c + 1],
                                        x_hi[:, c, :], c)
                        cut_lo(u + n + 2)
                        if n == KT // 2 - 2:
                            for c in range(KT - 2):
                                feed_lo(name, x_lo[:, c, :], h[:, c, :], gains[:, gain + c:gain + c + 1],
                                        x_hi[:, c, :], c)
                elif kind == "kv":
                    reciprocal_of_rms(fed_by[name], rstd[:])
                    for n in range(1 + HEADS):
                        dve.wait_ge(unit_done, u + n + 1)
                        if n == HEADS:
                            c = KT - 1
                            feed_lo(name, x_lo[:, c, :], h[:, c, :], gains[:, gain + c:gain + c + 1],
                                    x_hi[:, c, :], c)
                        if n == 0:
                            fx, ft, one = (t[0:HEADS, :] for t in (f_x, f_t, f_one))
                            nc.vector.memset(one, 1.0)
                            nc.vector.tensor_tensor(fx, ps[0:HEADS, bank_of(g), :], rstd[0:HEADS, :],
                                                    ALU.mult).then_inc(evac, 1)
                            dve.wait_ge(evac, g + 1)
                            nc.vector.tensor_scalar(fx, fx, small[0:HEADS, 2:3], None, op0=ALU.add).then_inc(f_d, 1)
                            cut_lo(u + 2)
                            dve.wait_ge(f_a, 3)
                            nc.vector.scalar_tensor_tensor(fx, fx, 0.0, ft, op0=ALU.min,
                                                           op1=ALU.subtract).then_inc(f_d, 1)
                            dve.wait_ge(f_d, 2)
                            nc.vector.tensor_tensor_scan(c_rows[0:HEADS, :], one, fx, 0.0, op0=ALU.mult,
                                                         op1=ALU.add).then_inc(f_d, 1)
                        else:
                            if n >= 3:
                                dve.wait_ge(kv_spilled[(n - 1) % 2], 16 * ((n - 1) // 2))
                            scaled(kv_out[(n - 1) % 2][:], g + n, 2, rstd[:])
                            cut_lo(u + n + 2)
                        if n == HEADS - 1:
                            for c in range(KT - 1):
                                feed_lo(name, x_lo[:, c, :], h[:, c, :], gains[:, gain + c:gain + c + 1],
                                        x_hi[:, c, :], c)
                elif kind == "foxin":
                    reciprocal_of_rms(fed_by[name], rstd[:])
                    for n in range(4):
                        dve.wait_ge(unit_done, u + n + 1)
                        scaled(fq[:, 2 * n:2 * n + 2, :] if n < 3 else fq_mem[:], g + n, 2, rstd[:])
                        if n < 3:
                            cut_lo(u + n + 2)
                        if n == 1:
                            dve.wait_ge(c_turned, 1)
                            nc.vector.tensor_copy(
                                c_cols[:, :, 0:HEADS],
                                ps[:, 4, 0:TT * 8].rearrange("p (t n) -> p t n", t=TT)[:, :, 0:HEADS]
                            ).then_inc(c_cols_ready, 1)
                        for hd in values_at[n]:
                            dve.wait_ge(fv_turned, hd + 1)
                            nc.vector.tensor_copy(fv[:, :, hd * P:(hd + 1) * P],
                                                  ps[:, 6 + hd % 2, :].rearrange("p (t n) -> p t n", t=TT)
                                                  ).then_inc(fv_ready, 1)
                        if n == 3:
                            cut_lo(u + n + 2)
                elif kind == "fox":
                    memory_attention(1, fq_mem)
                    for n in range(HEADS * TT + 5):
                        if n < HEADS * TT:
                            i = n % TT
                            w = (i + 1) * P
                            dve.wait_ge(f_score, n + 1)
                            dve.wait_ge(fb_masked, n + 1)
                            if n >= FOX_DEEP:
                                dve.wait_ge(f_turned, n - FOX_DEEP + 1)
                            nc.vector.scalar_tensor_tensor(fp[n % FOX_DEEP][:, 0:w], ps[:, 4 + n % 2, 0:w], HEAD ** -0.5,
                                                           bias_ts[n % 3][:, 0:w], op0=ALU.mult,
                                                           op1=ALU.add).then_inc(f_biased, 1)
                            dve.wait_ge(f_biased, n + 1)
                            nc.vector.tensor_reduce(f_stat[:, n % FOX_DEEP, 0:1], fp[n % FOX_DEEP][:, 0:w], AX_X, ALU.max,
                                                    negate=True).then_inc(f_max, 1)
                        if 2 <= n < HEADS * TT + 2:
                            m = n - 2
                            w = (m % TT + 1) * P
                            dve.wait_ge(f_exp, m + 1)
                            nc.vector.reciprocal(f_stat[:, m % FOX_DEEP, 2:3], f_stat[:, m % FOX_DEEP, 1:2]).then_inc(f_inv, 1)
                            dve.wait_ge(f_inv, m + 1)
                            nc.vector.tensor_scalar(fp[m % FOX_DEEP][:, 0:w], fp[m % FOX_DEEP][:, 0:w],
                                                    f_stat[:, m % FOX_DEEP, 2:3], None, op0=ALU.mult).then_inc(f_norm, 1)
                        if n >= 5 and (n - 5) % TT == TT - 1:
                            m = n - 5
                            dve.wait_ge(f_pv, m + 1)
                            hd = m // TT
                            nc.vector.tensor_copy(fq[:, hd, :], ps[:, 2 + hd % 2, :]).then_inc(f_out, 1)
                elif kind == "final":
                    for c in range(KT):
                        dve.wait_ge(y_turned, c + 1)
                        nc.vector.tensor_copy(y_tok[:, :, c * P:(c + 1) * P],
                                              ps[:, 6 + c % 2, :].rearrange("p (t n) -> p t n", t=TT)).then_inc(y_moved, 1)
                    dve.wait_ge(rms_ready, sums_before[last_update] + 1)
                    nc.vector.reciprocal(small[:, 4:8], small[:, 4:8]).then_inc(y_scale, 1)
                    dve.wait_ge(y_scale, 1)
                    dve.wait_ge(y_moved, KT)
                    for t in (0, 2):
                        nc.vector.tensor_scalar(y_tok[:, t, :], y_tok[:, t, :], small[:, 4 + t:5 + t],
                                                None, op0=ALU.mult).then_inc(y_ready, 1)

        @block.gpsimd
        def _(pool):
            made = [0]

            def constant(ins):
                made[0] += 1
                ins.then_inc(consts, 1)
                pool.wait_ge(consts, made[0])

            constant(nc.gpsimd.memset(ident[:], 0.0))
            constant(nc.gpsimd.affine_select(out=ident[:], in_=ident[:], compare_op=ALU.not_equal, fill=1.0,
                                             base=0, pattern=[[-1, P]], channel_multiplier=1))

            def add_square(name, b, c, tokens=SEQ, i=0):
                done = KT * sums_before[name] + c
                pool.wait_ge(sq_ready, done + 1 + 2 * i)
                if done >= 1:
                    pool.wait_ge(sum_ready, done + 2 * i)
                nc.gpsimd.tensor_tensor(square_sum[:, 0:tokens], square_sum[:, 0:tokens],
                                        gate_up[:, b, 0, 0:tokens], ALU.add).then_inc(sum_ready, 1)

            def clear_sum(name):
                n = sums_before[name]
                if n:
                    pool.wait_ge(sum_done, n)
                nc.gpsimd.memset(square_sum[:], 0.0).then_inc(sum_zero, 1)
                pool.wait_ge(sum_zero, n + 1)

            for name in phases:
                kind, idx = name[:-1], int(name[-1])
                if kind in ("memtr", "xtr"):
                    clear_sum(name)
                    for c in range(KT):
                        add_square(name, c % 2, c, MEM_LEN if kind == "memtr" else SEQ)
                elif kind == "up":
                    def step(n, j, i=0):
                        pool.wait_ge(silu_ready, NP * idx + n + 1 + 2 * i)
                        nc.gpsimd.tensor_tensor(gate_up[:, j, 0, :], gate_up[:, j, 0, :],
                                                gate_up[:, j, 1, :], ALU.mult).then_inc(prod_ready, 1)

                    with pool.Fori(0, NP // 2) as i:
                        for j in range(2):
                            step(j, j, i)
                elif kind == "down":
                    clear_sum(name)
                    with pool.Fori(0, KT // 2) as i:
                        for j in range(2):
                            add_square(name, j, j, i=i)
                elif kind == "gdnin":
                    pool.wait_ge(sum_done, sums_before[fed_by[name]])
                    pool.wait_ge(evac, first_group[name])
                    n_made = [0]

                    def constant2(ins):
                        n_made[0] += 1
                        ins.then_inc(mixer_consts, 1)
                        pool.wait_ge(mixer_consts, n_made[0])

                    def keep(dst, compare, base, pattern, multiplier, fill):
                        constant2(nc.gpsimd.affine_select(out=dst, in_=dst, compare_op=compare, fill=fill, base=base,
                                                          pattern=pattern, channel_multiplier=multiplier))

                    constant2(nc.gpsimd.memset(gate_rows[:], 0.0))
                    constant2(nc.gpsimd.memset(restart[:], 1.0))
                    constant2(nc.gpsimd.memset(restart[:].rearrange("p (c t) -> p c t", t=CHUNK)[:, :, 0:1], 0.0))
                    constant2(nc.gpsimd.memset(pick[:], 0.0))
                    for r0 in (0, ROW_B):
                        keep(pick[r0:r0 + ROW_B], ALU.not_equal, 0, [[-1, HEADS], [0, P]], 1, 1.0)
                    constant2(nc.gpsimd.memset(causal[:], 1.0))
                    keep(causal[:], ALU.is_ge, 0, [[1, P]], -1, 0.0)
                    constant2(nc.gpsimd.memset(causal[0:CHUNK, CHUNK:P], 0.0))
                    constant2(nc.gpsimd.memset(level[:], 1.0))
                    for l in range(HEADS):
                        s = 1 << l
                        dst = level[:, l, :].rearrange("p (a b) -> p a b", b=2 * s)
                        keep(dst, ALU.is_ge, 0, [[-2 * s, P // (2 * s)], [0, 2 * s]], 1, 0.0)
                        keep(dst, ALU.is_ge, s - 1, [[2 * s, P // (2 * s)], [0, 2 * s]], -1, 0.0)
                        constant2(nc.gpsimd.memset(dst[:, :, 0:s], 0.0))
                    assert n_made[0] == MIXER_CONSTS, n_made
                    qkv = [t[:, 2 * n:2 * n + 2, :] for t in (q, k) for n in range(HEADS // 2)]
                    for n in range(1, HEADS + 1):
                        pool.wait_ge(act_ready, n)
                        tiles = qkv[n - 1]
                        nc.gpsimd.tensor_tensor(sq[:], tiles, tiles, ALU.mult).then_inc(l2_sq, 1)
                        pool.wait_ge(l2_inv, n)
                        nc.gpsimd.tensor_tensor(tiles, tiles, sq[:], ALU.mult).then_inc(l2_done, 1)
                        pool.wait_ge(l2_done, n)
                    for hd in range(HEADS):
                        pool.wait_ge(decay_exp, hd + 1)
                        dst = decay[:, hd, :].rearrange("p (t n) -> p t n", t=TT)
                        nc.gpsimd.tensor_tensor(dst, dst, over_heads(causal[:], TT), ALU.mult).then_inc(decay_ready, 1)
                elif kind == "gdn":
                    def gate_output(p):
                        cs = pair_cols(p)
                        pool.wait_ge(o_scaled, p + 1)
                        nc.gpsimd.tensor_tensor(q[:, :, cs], o_pair[p % 2][:], z[:, :, cs], ALU.mult).then_inc(o_done, 1)

                    for p0 in range(0, TT, 2):
                        both = (p0, p0 + 1)
                        for p in both:
                            e = p % 2
                            pool.wait_ge(low_ready, p + 1)
                            if p >= 2:
                                pool.wait_ge(w_prod, p - 1)
                            nc.gpsimd.tensor_tensor(below[e][:], decay_beta[:, :, pair_cols(p)],
                                                    over_heads(level[:, 0, :]), ALU.mult).then_inc(below_step, 1)
                            pool.wait_ge(below_step, p + 1)
                            nc.gpsimd.tensor_tensor(inv_t[e][:], over_heads(ident[:]), below[e][:],
                                                    ALU.subtract).then_inc(inv0_ready, 1)
                        for lv in range(1, HEADS):
                            for p in both:
                                e, n, cs = p % 2, step_of(p, lv), pair_cols(p)
                                if lv == 1:
                                    pool.wait_ge(inv0_ready, p + 1)
                                else:
                                    pool.wait_ge(y_prod, n - 1)
                                nc.gpsimd.tensor_tensor(below[e][:], decay_beta[:, :, cs],
                                                        over_heads(level[:, lv, :]), ALU.mult).then_inc(below_ready, 1)
                                if lv == 2:
                                    pool.wait_ge(exp_g_ready, p + 1)
                                    pool.wait_ge(qk, p + 1)
                                    nc.gpsimd.tensor_tensor(q[:, :, cs], q[:, :, cs], exp_g[e][:],
                                                            ALU.mult).then_inc(q_head_ready, 1)
                                if lv == 3 and p0:
                                    gate_output(p - 2)
                        for n in range(2 * p0, 2 * p0 + 4):
                            p, c = divmod(n, 2)
                            if n:
                                pool.wait_ge(state_ready, n)
                                pool.wait_ge(o_prod, n)
                            else:
                                pool.wait_ge(state_zero, 1)
                            last_g = exp_g[p % 2][:, :, CHUNK * (c + 1) - 1:CHUNK * (c + 1)].broadcast_to(
                                [P, HEADS, P])
                            nc.gpsimd.tensor_tensor(state[(n + 1) % 2][:], state[n % 2][:], last_g,
                                                    ALU.mult).then_inc(state_decayed, 1)
                    gate_output(TT - 2)
                    gate_output(TT - 1)
                elif kind == "wout":
                    clear_sum(name)
                    for c in range(KT):
                        add_square(name, c % 2, c)
                elif kind == "kv":
                    for n in range(HEADS):
                        pool.wait_ge(evac, first_group[name] + n + 2)
                        pool.dma_start(kv_spill[:, 2 * n:2 * n + 2, :], kv_out[n % 2][:]).then_inc(kv_spilled[n % 2], 16)
                elif kind == "fox":
                    pool.wait_ge(evac, first_group["foxin0"] + 4)
                    nc.gpsimd.memset(fpick[:], 0.0).then_inc(fox_consts, 1)
                    pool.wait_ge(fox_consts, 1)
                    nc.gpsimd.affine_select(out=fpick[:], in_=fpick[:], compare_op=ALU.not_equal, fill=1.0,
                                            base=0, pattern=[[-1, HEADS], [0, P]],
                                            channel_multiplier=1).then_inc(fox_consts, 1)
                    for n in range(HEADS * TT):
                        i = n % TT
                        dst = bias_ts[n % 3][:, i * P:(i + 1) * P]
                        pool.wait_ge(fb_ready, n + 1)
                        nc.gpsimd.affine_select(out=dst, in_=dst, compare_op=ALU.is_ge, fill=NEG_INF, base=0,
                                                pattern=[[-1, P]], channel_multiplier=1).then_inc(fb_masked, 1)


_INS = ["mem", "x", "ffn1_norm", "ffn1_w_gate_up", "ffn1_w_down", "mix_norm", "ffn2_norm",
        "ffn2_w_gate_up", "ffn2_w_down", "gdn_w_in", "gdn_conv", "gdn_A_log", "gdn_dt_bias",
        "gdn_out_norm", "fox_w_in", "w_out", "mem_norm", "mem_w_kv", "kv_norm", "kv_w", "kv_b_f",
        "final_norm"]

PHASES = ["memtr0", "xtr0", "memkv0", "memkv1", "memvtr0", "up0", "down0", "gdnin0", "gdn0", "wout0",
          "up1", "down1", "kv0", "up2", "down2", "foxin0", "fox0", "wout1", "up3", "down3", "final0"]


def kernel(**inputs):
    import numpy as np
    import concourse.bacc as bacc
    from concourse.bass_utils import run_bass_kernel_spmd

    nc = bacc.Bacc("TRN2", target_bir_lowering=False, num_devices=1)
    arrays, args = {}, []
    for name in _INS:
        a = np.ascontiguousarray(inputs[name])
        arrays[f"in_{name}"] = a
        args.append(nc.dram_tensor(f"in_{name}", a.shape, mybir.dt.from_np(a.dtype), kind="ExternalInput").ap())
    kv_spill = nc.dram_tensor("kv_spill", (P, 2 * HEADS, SEQ), F32, kind="Internal").ap()
    out = nc.dram_tensor("out_0", (1, SEQ, D_MODEL), F32, kind="ExternalOutput").ap()
    build_trunk(nc, *args, kv_spill, out, PHASES)
    r = run_bass_kernel_spmd(nc, [arrays], core_ids=[0])
    return r.results[0]["out_0"]
```
